# Optimizing a Trainium2 kernel written in Bass

```python
import jax, jax.numpy as jnp
from jax import lax
import numpy as np

D_MODEL = 1024
BATCH = 1
SEQ = 256
DEPTH = 2

HEAD_DIM = 64
BRANCH_WIDTH = 256
N_HEADS_A = 4
IDX_HEADS = 4
IDX_DIM = 32
TOPK_MAX = 256
N_GROUPS_B = 4
GROUP_DIM_B = 64
CHUNK = 128
N_HEADS_C = 4
CONV_WIDTH = 3
Q_BLOCK = 128
ROPE_THETA = 10000.0
N_BRANCH = 4
N_EXPERT_GROUPS = 4
EXPERTS_PER_GROUP = 8
N_EXPERTS = N_EXPERT_GROUPS * EXPERTS_PER_GROUP
TOPK_IN_GROUP = 2
D_EXPERT = 256
MOE_BLOCK = 128
EPS = 1e-6

SPLIT_SIZES = (BRANCH_WIDTH, BRANCH_WIDTH, BRANCH_WIDTH,
               IDX_HEADS * IDX_DIM, IDX_DIM, IDX_HEADS,
               BRANCH_WIDTH, BRANCH_WIDTH,
               BRANCH_WIDTH, BRANCH_WIDTH, BRANCH_WIDTH,
               BRANCH_WIDTH, BRANCH_WIDTH, BRANCH_WIDTH,
               N_BRANCH * D_MODEL)
W_IN_COLS = sum(SPLIT_SIZES)

kernel_name = 'hybrid_gated_mixer_hmoe'

def rmsnorm(x, g):
    xf = x.astype(jnp.float32)
    y = xf * lax.rsqrt(jnp.mean(xf * xf, axis=-1, keepdims=True) + EPS)
    return (y * g.astype(jnp.float32)).astype(x.dtype)

def rope_tables(positions, dim):
    inv = ROPE_THETA ** (-jnp.arange(0, dim, 2, dtype=jnp.float32) / dim)
    ang = positions.astype(jnp.float32)[..., None] * inv
    return jnp.cos(ang)[:, :, None, :], jnp.sin(ang)[:, :, None, :]

def apply_rope(x, cos, sin):
    xf = x.astype(jnp.float32)
    x1, x2 = jnp.split(xf, 2, axis=-1)
    out = jnp.concatenate([x1 * cos - x2 * sin, x2 * cos + x1 * sin], axis=-1)
    return out.astype(x.dtype)

def to_blocks(a, nb):
    return jnp.moveaxis(a.reshape(a.shape[0], nb, Q_BLOCK, *a.shape[2:]), 1, 0)

def dsa_attention(q, k, v, iq, ik, iw):
    B, S, H, Dh = q.shape
    nb = S // Q_BLOCK
    topk = min(TOPK_MAX, S // 4)
    scale = Dh ** -0.5
    key_pos = jnp.arange(S)

    def block(args):
        qb, iqb, iwb, blk = args
        tq = blk * Q_BLOCK + jnp.arange(Q_BLOCK)
        causal = key_pos[None, :] <= tq[:, None]
        rel = jax.nn.relu(jnp.einsum('bqhd,bsd->bqhs', iqb, ik))
        score = jnp.einsum('bqh,bqhs->bqs', iwb, rel).astype(jnp.float32)
        score = jnp.where(causal[None], score, -jnp.inf)
        _, idx = lax.top_k(score, topk)
        valid = idx <= tq[None, :, None]
        k_sel = jax.vmap(lambda kb, ib: kb[ib])(k, idx)
        v_sel = jax.vmap(lambda vb, ib: vb[ib])(v, idx)
        logits = jnp.einsum('bqhd,bqkhd->bhqk', qb, k_sel).astype(jnp.float32) * scale
        logits = jnp.where(valid[:, None], logits, -jnp.inf)
        p = jax.nn.softmax(logits, axis=-1).astype(v.dtype)
        return jnp.einsum('bhqk,bqkhd->bqhd', p, v_sel)

    out = lax.map(block, (to_blocks(q, nb), to_blocks(iq, nb), to_blocks(iw, nb),
                          jnp.arange(nb)))
    return jnp.moveaxis(out, 0, 1).reshape(B, S, H * Dh)

def chunked_sgu(u, v, ln_g, ln_b, w_s, b_s):
    B, S, W = v.shape
    nc = S // CHUNK
    u = jax.nn.gelu(u)
    v = jax.nn.gelu(v)
    vf = v.astype(jnp.float32)
    mu = jnp.mean(vf, axis=-1, keepdims=True)
    var = jnp.mean(jnp.square(vf - mu), axis=-1, keepdims=True)
    vn = ((vf - mu) * lax.rsqrt(var + EPS) * ln_g + ln_b).astype(v.dtype)
    vn = vn.reshape(B, nc, CHUNK, N_GROUPS_B, GROUP_DIM_B)
    tril = jnp.tril(jnp.ones((CHUNK, CHUNK), dtype=w_s.dtype))
    mixed = jnp.einsum('gts,bcsgd->bctgd', w_s * tril, vn) + b_s.T[:, :, None]
    return u * mixed.reshape(B, S, W)

def stick_breaking_attention(q, k, v):
    B, S, H, Dh = q.shape
    nb = S // Q_BLOCK
    scale = Dh ** -0.5
    key_pos = jnp.arange(S)

    def block(args):
        qb, blk = args
        tq = blk * Q_BLOCK + jnp.arange(Q_BLOCK)
        strict = key_pos[None, :] < tq[:, None]
        z = jnp.einsum('bqhd,bshd->bhqs', qb, k).astype(jnp.float32) * scale
        log_beta = jax.nn.log_sigmoid(z)
        log_keep = jnp.where(strict, jax.nn.log_sigmoid(-z), 0.0)
        later = lax.cumsum(log_keep, axis=3, reverse=True) - log_keep
        a = jnp.where(strict, jnp.exp(log_beta + later), 0.0).astype(v.dtype)
        return jnp.einsum('bhqs,bshd->bqhd', a, v)

    out = lax.map(block, (to_blocks(q, nb), jnp.arange(nb)))
    return jnp.moveaxis(out, 0, 1).reshape(B, S, H * Dh)

def short_gated_conv(b_gate, c_gate, xin, conv_w):
    S = xin.shape[1]
    z = c_gate * xin
    zp = jnp.pad(z, ((0, 0), (CONV_WIDTH - 1, 0), (0, 0)))
    y = conv_w[0] * zp[:, 0:S]
    for tap in range(1, CONV_WIDTH):
        y = y + conv_w[tap] * zp[:, tap:tap + S]
    return b_gate * y

def token_mixers(h, cos_a, sin_a, cos_i, sin_i, w_in, ln_g, ln_b, w_s, b_s, conv_w,
                 w_branch, w_out):
    B, S, _ = h.shape
    proj = h @ w_in
    offsets = [int(o) for o in np.cumsum(SPLIT_SIZES)[:-1]]
    (qa, ka, va, iq, ik, iw, ub, vb, qc, kc, vc, bd, cd, xd,
     gate_logits) = jnp.split(proj, offsets, axis=-1)

    qa = apply_rope(qa.reshape(B, S, N_HEADS_A, HEAD_DIM), cos_a, sin_a)
    ka = apply_rope(ka.reshape(B, S, N_HEADS_A, HEAD_DIM), cos_a, sin_a)
    va = va.reshape(B, S, N_HEADS_A, HEAD_DIM)
    iq = apply_rope(iq.reshape(B, S, IDX_HEADS, IDX_DIM), cos_i, sin_i)
    ik = apply_rope(ik[:, :, None, :], cos_i, sin_i)[:, :, 0]
    y_a = dsa_attention(qa, ka, va, iq, ik, iw)

    y_b = chunked_sgu(ub, vb, ln_g, ln_b, w_s, b_s)

    y_c = stick_breaking_attention(qc.reshape(B, S, N_HEADS_C, HEAD_DIM),
                                   kc.reshape(B, S, N_HEADS_C, HEAD_DIM),
                                   vc.reshape(B, S, N_HEADS_C, HEAD_DIM))

    y_d = short_gated_conv(bd, cd, xd, conv_w)

    gates = jax.nn.sigmoid(gate_logits.astype(jnp.float32)).astype(h.dtype)
    gates = gates.reshape(B, S, N_BRANCH, D_MODEL)
    branches = (y_a, y_b, y_c, y_d)
    merged = gates[:, :, 0] * (branches[0] @ w_branch[0])
    for n in range(1, N_BRANCH):
        merged = merged + gates[:, :, n] * (branches[n] @ w_branch[n])
    return merged @ w_out

def hierarchical_moe(h, w_rg, b_rg, w_re, b_re, w_g, w_u, w_d):
    B, S, D = h.shape
    hf = h.astype(jnp.float32)
    p_grp = jax.nn.softmax(hf @ w_rg.astype(jnp.float32) + b_rg, axis=-1)
    grp_p, grp_idx = lax.top_k(p_grp, 1)
    exp_logits = (hf @ w_re.astype(jnp.float32) + b_re).reshape(
        B, S, N_EXPERT_GROUPS, EXPERTS_PER_GROUP)
    sel = jax.nn.one_hot(grp_idx[..., 0], N_EXPERT_GROUPS, dtype=jnp.float32)
    in_grp = jnp.einsum('bsg,bsge->bse', sel, exp_logits)
    top_l, top_j = lax.top_k(in_grp, TOPK_IN_GROUP)
    weights = grp_p * jax.nn.softmax(top_l, axis=-1)
    eid = grp_idx * EXPERTS_PER_GROUP + top_j
    combine = jnp.sum(jax.nn.one_hot(eid, N_EXPERTS, dtype=jnp.float32) * weights[..., None],
                      axis=2).astype(h.dtype)
    n_tok = B * S
    tok = h.reshape(n_tok // MOE_BLOCK, MOE_BLOCK, D)
    comb = combine.reshape(n_tok // MOE_BLOCK, MOE_BLOCK, N_EXPERTS)

    def block(args):
        tb, cb = args
        a = jnp.einsum('td,edf->tef', tb, w_g)
        u = jnp.einsum('td,edf->tef', tb, w_u)
        hh = jax.nn.silu(a) * u * cb[:, :, None]
        return jnp.einsum('tef,efd->td', hh, w_d)

    return lax.map(block, (tok, comb)).reshape(B, S, D)

def setup_inputs(seed: int = 0) -> dict:
    key = jax.random.key(seed)
    ks = jax.random.split(key, 19)

    def nrm(k, shape, fan):
        return jax.random.normal(k, shape, jnp.float32) * fan ** -0.5

    def noise(k, shape, s):
        return jax.random.normal(k, shape, jnp.float32) * s

    return {
        'x': jax.random.normal(ks[0], (BATCH, SEQ, D_MODEL), jnp.float32),
        'positions': jnp.broadcast_to(jnp.arange(SEQ, dtype=jnp.int32), (BATCH, SEQ)),
        'norm1_g': 1.0 + noise(ks[1], (DEPTH, D_MODEL), 0.02),
        'w_in': nrm(ks[2], (DEPTH, D_MODEL, W_IN_COLS), D_MODEL),
        'sgu_ln_g': 1.0 + noise(ks[3], (DEPTH, BRANCH_WIDTH), 0.02),
        'sgu_ln_b': noise(ks[4], (DEPTH, BRANCH_WIDTH), 0.02),
        'w_spatial': nrm(ks[5], (DEPTH, N_GROUPS_B, CHUNK, CHUNK), CHUNK),
        'b_spatial': 1.0 + noise(ks[6], (DEPTH, N_GROUPS_B, CHUNK), 0.1),
        'conv_w': nrm(ks[7], (DEPTH, CONV_WIDTH, BRANCH_WIDTH), CONV_WIDTH),
        'w_branch': nrm(ks[8], (DEPTH, N_BRANCH, BRANCH_WIDTH, D_MODEL), BRANCH_WIDTH),
        'w_out': nrm(ks[9], (DEPTH, D_MODEL, D_MODEL), D_MODEL),
        'norm2_g': 1.0 + noise(ks[10], (DEPTH, D_MODEL), 0.02),
        'w_router_group': nrm(ks[11], (DEPTH, D_MODEL, N_EXPERT_GROUPS), D_MODEL),
        'b_router_group': noise(ks[12], (DEPTH, N_EXPERT_GROUPS), 0.01),
        'w_router_expert': nrm(ks[13], (DEPTH, D_MODEL, N_EXPERTS), D_MODEL),
        'b_router_expert': noise(ks[14], (DEPTH, N_EXPERTS), 0.01),
        'w_exp_gate': nrm(ks[15], (DEPTH, N_EXPERTS, D_MODEL, D_EXPERT), D_MODEL),
        'w_exp_up': nrm(ks[16], (DEPTH, N_EXPERTS, D_MODEL, D_EXPERT), D_MODEL),
        'w_exp_down': nrm(ks[17], (DEPTH, N_EXPERTS, D_EXPERT, D_MODEL), D_EXPERT),
        'norm_f_g': 1.0 + noise(ks[18], (D_MODEL,), 0.02),
    }

def reference(x, positions, norm1_g, w_in, sgu_ln_g, sgu_ln_b, w_spatial, b_spatial, conv_w,
              w_branch, w_out, norm2_g, w_router_group, b_router_group, w_router_expert,
              b_router_expert, w_exp_gate, w_exp_up, w_exp_down, norm_f_g):
    cos_a, sin_a = rope_tables(positions, HEAD_DIM)
    cos_i, sin_i = rope_tables(positions, IDX_DIM)
    for l in range(DEPTH):
        h = rmsnorm(x, norm1_g[l])
        x = x + token_mixers(h, cos_a, sin_a, cos_i, sin_i, w_in[l], sgu_ln_g[l], sgu_ln_b[l],
                             w_spatial[l], b_spatial[l], conv_w[l], w_branch[l], w_out[l])
        h = rmsnorm(x, norm2_g[l])
        x = x + hierarchical_moe(h, w_router_group[l], b_router_group[l], w_router_expert[l],
                                 b_router_expert[l], w_exp_gate[l], w_exp_up[l], w_exp_down[l])
    return rmsnorm(x, norm_f_g)


_drawn_inputs = setup_inputs


def setup_inputs(seed=0):
    import zlib

    import numpy as np

    out = dict(_drawn_inputs(seed))
    spreads = {}
    factors = {'sgu_ln_g': 3.628, 'sgu_ln_b': 3.573, 'b_router_group': 4.051, 'norm_f_g': 2.908}
    for name, (base, spread) in spreads.items():
        noise = np.random.default_rng([zlib.crc32(name.encode()), seed]).standard_normal(out[name].shape)
        drawn = base * np.exp(spread * noise) if base else spread * noise
        out[name] = __import__('jax').numpy.asarray(drawn.astype(out[name].dtype))
    for name, factor in factors.items():
        out[name] = (out[name] * factor).astype(out[name].dtype)
    return out
```

```python
import math
from contextlib import ExitStack

import numpy as np
import concourse.bass as bass
from concourse import mybir

F32 = mybir.dt.float32
F32R = mybir.dt.float32r
I32 = mybir.dt.int32
ACT = mybir.ActivationFunctionType
ALU = mybir.AluOpType
AX = mybir.AxisListType

D = 1024
T = 256
DEPTH = 2
P = 128
TT = T // P
C = D // P
BW = 256
HD = 64
NH = 4
IH, ID = 4, 32
TOPK = min(256, T // 4)
NE, NG, EG = 32, 4, 8
DE = 256
EPS = 1e-6
ROPE_THETA = 10000.0
ATT_SCALE = HD ** -0.5
MASKED = -1.0e30
TAKEN = -3.0e38

BLOCK_VI = (512, 420)
BLOCK_QK = (0, 512)
BLOCK_QKC = (1444, 512)
BLOCK_VB = (1956, 512)
BLOCK_CX = (2468, 512)
BLOCK_UV = (932, 512)
GATES = 2980
BRANCH_ORDER = (3, 1, 2, 0)

MIXER_UNITS = [("in", b[0], b[1], h)
               for b in (BLOCK_VI, BLOCK_QK, BLOCK_QKC, BLOCK_VB, BLOCK_CX, BLOCK_UV) for h in range(2)]
for _n in BRANCH_ORDER:
    MIXER_UNITS.append(("branch", _n))
    MIXER_UNITS += [("in", GATES + _n * D + 512 * _hf, 512, _h) for _hf in range(2) for _h in range(2)]
MIXER_UNITS += [("out", _u) for _u in range(4)]
NU = len(MIXER_UNITS)
LAST_UNIT = [1, 3, 5, 7, 9, 11]
for _j in range(4):
    LAST_UNIT += [12 + 5 * _j, 12 + 5 * _j, 14 + 5 * _j, 16 + 5 * _j]
RING = 12
MRING = 9
UNIT = 2048
HALF = UNIT // 2
SPLITS = 4
GE = 4
GROUPS = NE // GE
SLOTS = 32
LOADS_LOW = NU // MRING + GROUPS
LOADS_HIGH = GROUPS
MAXPASS = T // SLOTS

PG1, PG2, PBS, PCW, PBR = 0, C, 2 * C, 2 * C + 4, 2 * C + 10
NSMALL = PBR + NG + NE


def build(nc, x_in, positions, norm1_g, w_in, sgu_ln_g, sgu_ln_b, w_spatial, b_spatial, conv_w, w_branch,
          w_out, norm2_g, w_rg, b_rg, w_re, b_re, w_eg, w_eu, w_ed, norm_f_g, out):
    ctx = ExitStack()
    with ctx:
        def sb(name, shape, dt=F32):
            return ctx.enter_context(nc.sbuf_tensor(name, shape, dt))

        ring = sb("ring", [P, RING * UNIT])
        split_hi = sb("split_hi", [P, SPLITS, HALF], F32R)
        split_lo = sb("split_lo", [P, SPLITS, HALF], F32R)
        x = sb("x", [P, TT, D])
        hT_hi = sb("hT_hi", [P, C, T], F32R)
        hT_lo = sb("hT_lo", [P, C, T], F32R)
        yT_hi = sb("yT_hi", [P, 2, 2, T], F32R)
        yT_lo = sb("yT_lo", [P, 2, 2, T], F32R)
        wide = sb("wide", [P, TT, D])
        qkr = sb("qkr", [P, TT, 512])
        tmpP = sb("tmpP", [P, TT, 512])
        idx = sb("idx", [P, TT, 256])
        br = sb("br", [P, 2, TT, 512])
        y_ab = sb("y_ab", [P, TT, BW])
        y_c = sb("y_c", [P, TT, BW])
        vc = sb("vc", [P, TT, BW])
        mb = sb("mb", [P, 384])
        small_all = sb("small_all", [P, DEPTH, NSMALL])
        small = sb("small", [P, NSMALL])
        lnp = sb("lnp", [P, 2, BW])
        ws = y_c[:, :, :].rearrange("p t n -> p (t n)").rearrange("p (g s) -> p g s", g=NG)
        wsT = sb("wsT", [P, NG, P])
        wr = sb("wr", [P, C, NG + NE])
        ident = sb("ident", [P, P])
        ones = sb("ones", [P, P])
        strict_T = sb("strict_T", [P, P])
        incl_T = sb("incl_T", [P, P])
        mask_a = sb("mask_a", [P, 2 * P])
        mask_c = sb("mask_c", [P, 2 * P])
        cos_a, sin_a = sb("cos_a", [P, TT, HD]), sb("sin_a", [P, TT, HD])
        cos_i, sin_i = sb("cos_i", [P, TT, ID]), sb("sin_i", [P, TT, ID])
        pos_i = sb("pos_i", [P, TT], I32)
        slot_no = sb("slot_no", [P, SLOTS])
        slot_cur = sb("slot_cur", [P, SLOTS])
        desc = sb("desc", [P, EG])
        limits = sb("limits", [P, MAXPASS - 1])
        scal = sb("scal", [P, 64])
        npass = sb("npass", [1, GROUPS], I32)
        bn = sb("bn", [P, TT, 6])
        wt = sb("wt", [P, TT, NE])
        rankm = sb("rankm", [P, TT, NE])

        def att(k):
            return ring[:, (MRING * 2 + k) * HALF:(MRING * 2 + k + 1) * HALF]
        qkT_a = att(0).rearrange("p (m t) -> p m t", m=4)
        zc = att(1).rearrange("p (h s) -> p h s", h=NH)
        sc = att(2).rearrange("p (h s) -> p h s", h=NH)
        pT = att(3).rearrange("p (b h q) -> p b h q", b=2, h=NH)
        uv = att(4).rearrange("p (t n) -> p t n", t=TT)
        vi = att(5)[:, 0:TT * 420].rearrange("p (t n) -> p t n", t=TT)
        iqT = br[:, 0, :, :].rearrange("p a n -> p (a n)").rearrange("p (h t) -> p h t", h=IH)
        qkT_c = br[:, 1, :, :].rearrange("p a n -> p (a n)").rearrange("p (m t) -> p m t", m=4)
        bdT = wide[:, 0, 0:512].rearrange("p (m t) -> p m t", m=2)
        ikT = wide[:, 0, 512:768]
        score = wide[:, 1, 0:256]
        cxT = tmpP[:, :, :].rearrange("p a n -> p (a n)").rearrange("p (m t) -> p m t", m=4)
        sig = qkr
        merged = wide
        vn = idx
        xn_hi = split_hi[:, 0:2, :]
        xn_lo = split_lo[:, 0:2, :]
        pick = split_hi[:, 2, 0:TT * P].rearrange("p (t s) -> p t s", t=TT)
        wr_hi = split_hi[:, 3, 0:C * (NG + NE)].rearrange("p (c e) -> p c e", c=C)
        wr_lo = split_lo[:, 3, 0:C * (NG + NE)].rearrange("p (c e) -> p c e", c=C)
        hG = qkr[:, :, :].rearrange("p a n -> p (a n)").rearrange("p (c s) -> p c s", c=C)
        y_slots = tmpP[:, :, :].rearrange("p a n -> p (a n)")
        brf = br[:, :, :, :].rearrange("p a b n -> p (a b n)")
        wpick = brf[:, 0:256].rearrange("p (t s) -> p t s", t=TT)
        scatT = brf[:, 256:512].rearrange("p (t s) -> p t s", t=TT)
        hid = brf[0:SLOTS, 512:1024].rearrange("p (a f) -> p a f", a=2)
        silu = brf[:, 1024:1152].rearrange("p (a f) -> p a f", a=2)
        hidT = brf[:, 1152:1280].rearrange("p (a k s) -> p a k s", a=2, k=2)
        rl = brf[:, 1280:1280 + TT * 36].rearrange("p (t e) -> p t e", t=TT)
        member = brf[:, 1408:1472].rearrange("p (t e) -> p t e", t=TT)
        prod32 = brf[:, 1472:1536].rearrange("p (t g e) -> p t g e", t=TT, g=NG)
        rt = brf[:, 1536:1792]
        cnts = brf[:, 1792:1856]

        ps = ctx.enter_context(nc.psum_tensor("ps", [P, 8, 512], F32))

        def sem(name):
            return ctx.enter_context(nc.semaphore(name))

        ring_loaded = [sem(f"ring_loaded{i}") for i in range(RING)]
        once_loaded = sem("once_loaded")
        layer_loaded = sem("layer_loaded")
        out_stored = sem("out_stored")
        tab = sem("tab")
        first = sem("layer_first")
        hi_done, lo_done, half_used = sem("hi_done"), sem("lo_done"), sem("half_used")
        small_ready = sem("small_ready")
        squares, var_ready, root, inv_rms = sem("squares"), sem("var_ready"), sem("root"), sem("inv_rms")
        xn_dve, xn_act = sem("xn_dve"), sem("xn_act")
        xT_mm, xT_hi, xT_lo = sem("xT_mm"), sem("xT_hi"), sem("xT_lo")
        ws_T, ws_ready = sem("ws_T"), sem("ws_ready")
        block_out = sem("block_out")
        rot_i, rot_a, pool_c = sem("rot_i"), sem("rot_a"), sem("pool_c")
        idx_T, idx_out, rel_mm, rel_out = sem("idx_T"), sem("idx_out"), sem("rel_mm"), sem("rel_out")
        qk_T, qk_out, mb_done = sem("qk_T"), sem("qk_out"), sem("mb_done")
        zc_mm, zc_out, zabs, zln, zarg, zexp = (sem("zc_mm"), sem("zc_out"), sem("zabs"), sem("zln"),
                                               sem("zarg"), sem("zexp"))
        pT_mm, pT_out, pv_mm, y_out = sem("pT_mm"), sem("pT_out"), sem("pv_mm"), sem("y_out")
        conv_y, gelu_out = sem("conv_y"), sem("gelu_out")
        ln_var, ln_root, vn_dve, vn_done = sem("ln_var"), sem("ln_root"), sem("vn_dve"), sem("vn_done")
        sgu_mm, yb_done = sem("sgu_mm"), sem("yb_done")
        yT_mm, yT_hi_out, yT_lo_out = sem("yT_mm"), sem("yT_hi_out"), sem("yT_lo_out")
        la_mm, la_out, la_max, la_exp, la_sum = (sem("la_mm"), sem("la_out"), sem("la_max"), sem("la_exp"),
                                                sem("la_sum"))
        gate_prod, gate_sum = sem("gate_prod"), sem("gate_sum")
        x_mid = sem("x_mid")
        wr_hi_out, wr_lo_out, route_mm = sem("wr_hi_out"), sem("wr_lo_out"), sem("route_mm")
        xs_hi, xs_lo = sem("xs_hi"), sem("xs_lo")
        gmax, gexp, emax, eexp = sem("gmax"), sem("gexp"), sem("emax"), sem("eexp")
        member_ok, rank_mm, passes_ok, routed = (sem("member_ok"), sem("rank_mm"), sem("passes_ok"),
                                                 sem("routed"))
        dve_c = sem("dve_c")
        pick_ok, wpick_ok, slot_c = sem("pick_ok"), sem("wpick_ok"), sem("slot_c")
        gath_mm, gath_out = sem("gath_mm"), sem("gath_out")
        scat_T, scat_T_out = sem("scat_T"), sem("scat_T_out")
        gu_mm, silu_out, hid_out, hid_T, hidT_out = (sem("gu_mm"), sem("silu_out"), sem("hid_out"),
                                                     sem("hid_T"), sem("hidT_out"))
        down_mm, y_act, y_dve = sem("down_mm"), sem("y_act"), sem("y_dve")
        scat_mm, x_add = sem("scat_mm"), sem("x_add")
        unit_used = sem("unit_used")
        last = sem("layer_last")

        w_in_v = w_in.rearrange("l (p c) n -> l p c n", c=C)
        w_br_v = w_branch.rearrange("l b (k p) n -> l b p k n", p=P)
        w_out_v = w_out.rearrange("l (c p) n -> l p c n", p=P)
        w_eg_v = w_eg.rearrange("l e (p c) f -> (l e) p c f", c=C)
        w_eu_v = w_eu.rearrange("l e (p c) f -> (l e) p c f", c=C)
        w_ed_v = w_ed.rearrange("l e (p k) d -> (l e) p k d", k=2)

        def slot(s):
            return ring[:, s * UNIT:(s + 1) * UNIT]

        def unit_cols(u):
            return MIXER_UNITS[u][2] if MIXER_UNITS[u][0] == "in" else D

        def half_view(buf, v):
            n = unit_cols(v // 2)
            if n == D:
                return buf.rearrange("p (k n) -> p k n", k=1)
            return buf.rearrange("p (k n) -> p k n", k=2)[:, :, 0:n]

        def raw_half(v):
            s = (v // 2) % MRING
            return half_view(ring[:, s * UNIT + (v % 2) * HALF:s * UNIT + (v % 2 + 1) * HALF], v)

        def load_mixer_unit(sp, u, l):
            kind = MIXER_UNITS[u]
            s = u % MRING
            if kind[0] == "in":
                _, c0, n, h = kind
                dst = slot(s).rearrange("p (k n) -> p k n", k=4)[:, :, 0:n]
                src = w_in_v[l][:, 4 * h:4 * h + 4, c0:c0 + n]
            elif kind[0] == "branch":
                dst = slot(s).rearrange("p (k n) -> p k n", k=2)
                src = w_br_v[l][kind[1]]
            else:
                dst = slot(s).rearrange("p (k n) -> p k n", k=2)
                src = w_out_v[l][:, 2 * kind[1]:2 * kind[1] + 2, :]
            sp.dma_start(dst, src).then_inc(ring_loaded[s], 16)

        def load_expert_unit(sp, le, i, part):
            s = 3 * i + part
            if part < 2:
                dst = slot(s).rearrange("p (c f) -> p c f", c=C)
                src = (w_eg_v if part == 0 else w_eu_v)[le]
            else:
                dst = slot(s).rearrange("p (k d) -> p k d", k=2)
                src = w_ed_v[le]
            sp.dma_start(dst, src).then_inc(ring_loaded[s], 16)

        inv_freq = (ROPE_THETA ** (-np.arange(0, HD, 2) / HD)).astype(np.float32)
        NONCE = 2 + 7 * DEPTH
        ang, red, freq = brf[:, 0:64], brf[:, 64:128], brf[:, 128:160]
        posf = scal[:, 0:TT]
        with nc.Block() as once:

            @once.sync
            def _(sp):
                sp.dma_start(x[:], x_in[0].rearrange("(t p) d -> p t d", p=P)).then_inc(once_loaded, 16)
                sp.dma_start(pos_i[:], positions[0].rearrange("(t p) -> p t", p=P),
                             allow_slow_non_contiguous=True).then_inc(once_loaded, 16)
                for u in range(MRING):
                    load_mixer_unit(sp, u, 0)

            @once.scalar
            def _(act):
                for l in range(DEPTH):
                    for at, src in ((PG1, norm1_g[l].rearrange("(p c) -> p c", c=C)),
                                    (PG2, norm2_g[l].rearrange("(p c) -> p c", c=C)),
                                    (PBS, b_spatial[l].rearrange("g t -> t g"))):
                        w = src.shape[1]
                        act.dma_start(small_all[:, l, at:at + w], src, allow_slow_non_contiguous=True).then_inc(once_loaded, 16)
                    for k in range(2):
                        act.dma_start(small_all[:, l, PCW + 3 * k:PCW + 3 * k + 3],
                                      conv_w[l][:, P * k:P * k + P].rearrange("w p -> p w"),
                                      allow_slow_non_contiguous=True)\
                           .then_inc(once_loaded, 16)
                    act.dma_start(small_all[:, l, PBR:PBR + NG],
                                  b_rg[l:l + 1, :].broadcast_to([P, NG])).then_inc(once_loaded, 16)
                    act.dma_start(small_all[:, l, PBR + NG:PBR + NG + NE],
                                  b_re[l:l + 1, :].broadcast_to([P, NE])).then_inc(once_loaded, 16)
                act.wait_ge(tab, 1)
                nc.scalar.activation(ang, ang, ACT.Sin).then_inc(tab, 1)
                nc.scalar.activation(red, red, ACT.Sin).then_inc(tab, 1)

            @once.gpsimd
            def _(pool):
                for i in range(HD // 2):
                    nc.gpsimd.memset(freq[:, i:i + 1], float(inv_freq[i]))
                for i in range(EG):
                    nc.gpsimd.memset(desc[:, i:i + 1], float(EG - i))
                for i in range(MAXPASS - 1):
                    nc.gpsimd.memset(limits[:, i:i + 1], float(SLOTS * (i + 1)))
                nc.gpsimd.memset(mask_a[:], 0.0)
                nc.gpsimd.memset(mask_c[:], 0.0)
                nc.gpsimd.memset(ones[:], 1.0).then_inc(pool_c, 1)
                pool.wait_ge(pool_c, 1)
                nc.gpsimd.iota(slot_no[:], pattern=[[1, SLOTS]], base=0, channel_multiplier=0,
                               allow_small_or_imprecise_dtypes=True)
                nc.gpsimd.affine_select(out=ident[:], in_=ones[:], compare_op=ALU.is_equal, fill=0.0, base=0,
                                        pattern=[[-1, P]], channel_multiplier=1)
                nc.gpsimd.affine_select(out=strict_T[:], in_=ones[:], compare_op=ALU.is_gt, fill=0.0, base=0,
                                        pattern=[[1, P]], channel_multiplier=-1)
                nc.gpsimd.affine_select(out=incl_T[:], in_=ones[:], compare_op=ALU.is_ge, fill=0.0, base=0,
                                        pattern=[[1, P]], channel_multiplier=-1)
                nc.gpsimd.affine_select(out=mask_a[:, P:], in_=mask_a[:, P:], compare_op=ALU.is_ge, fill=MASKED,
                                        base=0, pattern=[[-1, P]], channel_multiplier=1)
                nc.gpsimd.affine_select(out=mask_c[:, P:], in_=mask_c[:, P:], compare_op=ALU.is_gt, fill=MASKED,
                                        base=0, pattern=[[-1, P]], channel_multiplier=1).then_inc(pool_c, 1)

            @once.vector
            def _(dve):
                n = [0]

                def link(ins):
                    n[0] += 1
                    ins.then_inc(dve_c, 1)
                    dve.wait_ge(dve_c, n[0])

                dve.wait_ge(once_loaded, 16 * NONCE)
                dve.wait_ge(pool_c, 2)
                link(nc.vector.tensor_copy(posf, pos_i[:]))
                for t in range(TT):
                    link(nc.vector.tensor_scalar(ang[:, 32 * t:32 * t + 32], freq, posf[:, t:t + 1], None,
                                                 ALU.mult))
                magic = 12582912.0
                c1, c2 = 6.28125, 0.0019350051879882812
                c3 = 2 * math.pi - c1 - c2
                link(nc.vector.tensor_scalar(red, ang, 1 / (2 * math.pi), magic, ALU.mult, ALU.add))
                link(nc.vector.tensor_scalar(red, red, magic, None, ALU.subtract))
                for c in (c1, c2, c3):
                    link(nc.vector.scalar_tensor_tensor(ang, red, -c, ang, ALU.mult, ALU.add))
                link(nc.vector.tensor_scalar(ang, ang, 3.141592, -3.141592, ALU.min, ALU.max))
                link(nc.vector.tensor_scalar(red, ang, math.pi / 2, None, ALU.add))
                tmp = brf[:, 160:224]
                link(nc.vector.tensor_scalar(tmp, red, math.pi, 2 * math.pi, ALU.is_gt, ALU.mult))
                link(nc.vector.tensor_tensor(red, red, tmp, ALU.subtract))
                link(nc.vector.tensor_scalar(red, red, 3.141592, -3.141592, ALU.min, ALU.max))
                nc.vector.tensor_scalar(posf, posf, 1.0, None, ALU.mult).then_inc(tab, 1)
                dve.wait_ge(tab, 3)
                s3 = ang.rearrange("p (t f) -> p t f", t=TT)
                c3_ = red.rearrange("p (t f) -> p t f", t=TT)
                for h in range(2):
                    nc.vector.tensor_copy(cos_a[:, :, 32 * h:32 * h + 32], c3_)
                    nc.vector.tensor_scalar(sin_a[:, :, 32 * h:32 * h + 32], s3, 2.0 * h - 1.0, None, ALU.mult)
                    nc.vector.tensor_copy(cos_i[:, :, 16 * h:16 * h + 16], c3_[:, :, ::2])
                    nc.vector.tensor_scalar(sin_i[:, :, 16 * h:16 * h + 16], s3[:, :, ::2], 2.0 * h - 1.0, None,
                                            ALU.mult)
        nc.gpsimd.sem_clear(range(first.num, last.num + 1))
        nc.all_engine_barrier()

        ss, var, sd, ir, nt = (scal[:, 2 * i:2 * i + 2] for i in range(5))
        top8 = scal[:, 16:24]
        lmax, lneg, lsum, linv = (scal[:, 24 + 4 * i:28 + 4 * i] for i in range(4))
        lmv = scal[:, 40:44].rearrange("p (t k) -> p t k", t=TT)
        lvar, lsd, lrs = scal[:, 44:46], scal[:, 46:48], scal[:, 48:50]
        xp = [x[:, t, :].rearrange("p (q c) -> p c q", c=C) for t in range(TT)]
        xnp = [wide[:, t, :].rearrange("p (c q) -> p c q", c=C) for t in range(TT)]

        def bank(b, n=1):
            return ps[:, b, :] if n == 1 else ps[:, b:b + n, :]

        with nc.Fori(0, DEPTH) as l:
            with nc.Block() as layer:

                @layer.sync
                def _(sp):
                    for u in range(MRING, NU):
                        sp.wait_ge(lo_done, 2 * (u - MRING + 1))
                        load_mixer_unit(sp, u, l)
                    for i in range(GE):
                        for part in range(3):
                            s = 3 * i + part
                            if s < MRING:
                                sp.wait_ge(lo_done, 2 * (NU - MRING + s + 1))
                            elif s == MRING:
                                sp.wait_ge(pv_mm, 4)
                            load_expert_unit(sp, l * NE + i, i, part)
                    with sp.Fori(1, GROUPS) as g:
                        for i in range(GE):
                            for part in range(3):
                                sp.wait_ge(unit_used, g * RING + (3 * i + part + 1 - RING))
                                load_expert_unit(sp, l * NE + g * GE + i, i, part)
                    with sp.If(l < DEPTH - 1):
                        after = nc.s_assert_within(l + 1, 0, DEPTH - 1, skip_runtime_bounds_check_because=
                                                   "only where a layer follows")
                        for u in range(MRING):
                            sp.wait_ge(unit_used, (GROUPS - 1) * RING + u + 1)
                            load_mixer_unit(sp, u, after)

                @layer.gpsimd
                def _(pool):
                    n = [0]

                    def link(ins):
                        n[0] += 1
                        ins.then_inc(pool_c, 1)
                        return n[0]

                    for k, src in enumerate((sgu_ln_g, sgu_ln_b)):
                        pool.dma_start(lnp[:, k, :], src[l].rearrange("(o n) -> o n", o=1)
                                       .broadcast_to([P, BW])).then_inc(layer_loaded, 16)
                    pool.dma_start(ws, w_spatial[l].rearrange("g t s -> t g s")).then_inc(layer_loaded, 16)
                    pool.dma_start(wr[:, :, 0:NG], w_rg[l].rearrange("(p c) e -> p c e", c=C))\
                        .then_inc(layer_loaded, 16)
                    pool.dma_start(wr[:, :, NG:], w_re[l].rearrange("(p c) e -> p c e", c=C))\
                        .then_inc(layer_loaded, 16)
                    nc.gpsimd.memset(iqT, 0.0).then_inc(first, 1)

                    pool.wait_ge(block_out, 1)
                    H5 = IH + 1
                    for t in range(TT):
                        src = vi[:, t, 256:416].rearrange("p (h s f) -> p h s f", h=H5, s=2)
                        full = vi[:, t, 256:416].rearrange("p (h f) -> p h f", h=H5)
                        a = tmpP[:, t, 0:160].rearrange("p (h f) -> p h f", h=H5)
                        b = tmpP[:, t, 160:320].rearrange("p (h s f) -> p h s f", h=H5, s=2)
                        bf = tmpP[:, t, 160:320].rearrange("p (h f) -> p h f", h=H5)
                        nc.gpsimd.tensor_tensor(a, full, cos_i[:, t:t + 1, :].broadcast_to([P, H5, ID]), ALU.mult)
                        nc.gpsimd.tensor_tensor(b[:, :, 0, :], src[:, :, 1, :],
                                                sin_i[:, t:t + 1, 0:16].broadcast_to([P, H5, 16]), ALU.mult)
                        k = link(nc.gpsimd.tensor_tensor(b[:, :, 1, :], src[:, :, 0, :],
                                                         sin_i[:, t:t + 1, 16:32].broadcast_to([P, H5, 16]),
                                                         ALU.mult))
                        pool.wait_ge(pool_c, k)
                        nc.gpsimd.tensor_tensor(idx[:, t, 0:128].rearrange("p (h f) -> p h f", h=IH),
                                                a[:, 0:IH, :], bf[:, 0:IH, :], ALU.add)
                        nc.gpsimd.tensor_tensor(idx[:, t, 128:256].rearrange("p (h f) -> p h f", h=IH),
                                                a[:, IH:H5, :].broadcast_to([P, IH, ID]),
                                                bf[:, IH:H5, :].broadcast_to([P, IH, ID]), ALU.add)\
                            .then_inc(rot_i, 1)
                    pool.wait_ge(block_out, 2)
                    pool.wait_ge(rot_i, 2)
                    H8 = 2 * NH
                    for t in range(TT):
                        src = uv[:, t, :].rearrange("p (h s f) -> p h s f", h=H8, s=2)
                        full = uv[:, t, :].rearrange("p (h f) -> p h f", h=H8)
                        a = tmpP[:, t, :].rearrange("p (h f) -> p h f", h=H8)
                        b = qkr[:, t, :].rearrange("p (h s f) -> p h s f", h=H8, s=2)
                        nc.gpsimd.tensor_tensor(a, full, cos_a[:, t:t + 1, :].broadcast_to([P, H8, HD]), ALU.mult)
                        nc.gpsimd.tensor_tensor(b[:, :, 0, :], src[:, :, 1, :],
                                                sin_a[:, t:t + 1, 0:32].broadcast_to([P, H8, 32]), ALU.mult)
                        k = link(nc.gpsimd.tensor_tensor(b[:, :, 1, :], src[:, :, 0, :],
                                                         sin_a[:, t:t + 1, 32:64].broadcast_to([P, H8, 32]),
                                                         ALU.mult))
                        pool.wait_ge(pool_c, k)
                        nc.gpsimd.tensor_tensor(qkr[:, t, :], tmpP[:, t, :], qkr[:, t, :], ALU.add)\
                            .then_inc(rot_a, 1)
                    pool.wait_ge(layer_loaded, 16 * 5 * (l + 1))
                    pool.wait_ge(vn_dve, 1)
                    k = link(nc.gpsimd.tensor_tensor(vn[:], vn[:], lnp[:, 0:1, :].broadcast_to([P, TT, BW]),
                                                     ALU.mult))
                    pool.wait_ge(pool_c, k)
                    nc.gpsimd.tensor_tensor(vn[:], vn[:], lnp[:, 1:2, :].broadcast_to([P, TT, BW]), ALU.add)\
                        .then_inc(vn_done, 1)
                    for j in range(2, 7):
                        hf = j % 2
                        pool.wait_ge(gate_prod, j + 1)
                        m = merged[:, :, 512 * hf:512 * hf + 512]
                        nc.gpsimd.tensor_tensor(m, m, sig[:], ALU.add).then_inc(gate_sum, 1)

                @layer.tensor
                def _(pe):
                    mm = nc.tensor.matmul

                    def transposes(dsts, srcs, done, idn=None):
                        for k, (d_, s_) in enumerate(zip(dsts, srcs)):
                            ins = nc.tensor.transpose(d_, s_, ident[:] if idn is None else idn)
                        ins.then_inc(done, 1)

                    def three(dst, st, mv, start, stop):
                        mm(dst, st[0], mv[0], start=start, stop=False, skip_group_check=True)
                        mm(dst, st[0], mv[1], start=False, stop=False, skip_group_check=True)
                        return mm(dst, st[1], mv[0], start=False, stop=stop, skip_group_check=True)

                    def h_tile(c, t=None):
                        cols = slice(0, T) if t is None else slice(P * t, P * t + P)
                        return hT_hi[:, c, cols], hT_lo[:, c, cols]

                    def w_tile(v, k, c0, n):
                        return (half_view(split_hi[:, v % SPLITS, :], v)[:, k, c0:c0 + n],
                                half_view(split_lo[:, v % SPLITS, :], v)[:, k, c0:c0 + n])

                    def in_half(v, use, layout):
                        b0 = 2 * (use % 2)
                        h = MIXER_UNITS[v // 2][3]
                        n = unit_cols(v // 2)
                        pe.wait_ge(lo_done, v + 1)
                        chunks = [(4 * h + 2 * (v % 2) + k, k) for k in range(2)]
                        begin, end = chunks[0][0] == 0, chunks[-1][0] == C - 1
                        if begin and use >= 2:
                            pe.wait_ge(block_out, use - 1)
                        outs = []
                        if layout == "natural":
                            for t in range(TT):
                                outs.append((ps[:, b0 + t, 0:n], lambda c, k, t=t: h_tile(c, t),
                                             lambda c, k: w_tile(v, k, 0, n), True))
                        elif layout == "transposed":
                            for m in range(4):
                                outs.append((ps[:, b0 + m // 2, T * (m % 2):T * (m % 2) + T],
                                             lambda c, k, m=m: w_tile(v, k, P * m, P),
                                             lambda c, k: h_tile(c), m % 2 == 0))
                        else:
                            for t in range(TT):
                                outs.append((ps[:, b0, BW * t:BW * t + BW], lambda c, k, t=t: h_tile(c, t),
                                             lambda c, k: w_tile(v, k, 0, BW), t == 0))
                            for m in range(2):
                                outs.append((ps[:, b0 + 1, T * m:T * m + T],
                                             lambda c, k, m=m: w_tile(v, k, BW + P * m, P),
                                             lambda c, k: h_tile(c), m == 0))
                        for dst, st, mv, opens in outs:
                            for c, k in chunks:
                                ins = three(dst, st(c, k), mv(c, k), begin and k == 0 and opens,
                                            end and k == 1)
                        ins.then_inc(half_used, 1)

                    def in_unit(u, use, layout="natural"):
                        in_half(2 * u, use, layout)
                        in_half(2 * u + 1, use, layout)

                    def wide_unit(u, use, st, first_, last_):
                        for v in (2 * u, 2 * u + 1):
                            pe.wait_ge(lo_done, v + 1)
                            for hf in range(2):
                                if first_ and v % 2 == 0:
                                    pe.wait_ge(block_out, use + hf - 1)
                                for t in range(TT):
                                    ins = three(ps[:, 2 * hf + t, :], st(v % 2, t), w_tile(v, 0, 512 * hf, 512),
                                                first_ and v % 2 == 0, last_ and v % 2 == 1)
                            ins.then_inc(half_used, 1)

                    def x_transposes(done0):
                        for b in range(4):
                            transposes([ps[:, 4 + b, T * k + P * t:T * k + P * t + P]
                                        for k in range(2) for t in range(TT)],
                                       [wide[:, t, P * (2 * b + k):P * (2 * b + k) + P]
                                        for k in range(2) for t in range(TT)], xT_mm)

                    def logits(qk, t, b0, done):
                        w = P * (t + 1)
                        for m in range(2):
                            for r in range(2):
                                ins = mm(ps[:, b0 + r, 256 * m:256 * m + w],
                                         qk[HD * r:HD * r + HD, m, P * t:P * t + P],
                                         qk[HD * r:HD * r + HD, 2 + m, 0:w], start=(m == 0), stop=True,
                                         skip_group_check=True)
                        ins.then_inc(done, 1)

                    def p_transposes(src, t, b0):
                        for b in range(t + 1):
                            for h in range(NH):
                                ins = nc.tensor.transpose(ps[:, b0 + b, P * h:P * h + P],
                                                          src[:, h, P * b:P * b + P], ident[:])
                        ins.then_inc(pT_mm, 1)

                    def pv(v, t, b0):
                        for s_, h in enumerate((0, 2, 1, 3)):
                            for b in range(t + 1):
                                ins = mm(ps[:, b0, HD * h:HD * h + HD], pT[:, b, s_, :],
                                         v[:, b, HD * h:HD * h + HD], start=(b == 0), stop=(b == t),
                                         skip_group_check=True)
                        ins.then_inc(pv_mm, 1)

                    def y_transposes(y, b0):
                        transposes([ps[:, b0, T * k + P * t:T * k + P * t + P]
                                    for k in range(2) for t in range(TT)],
                                   [y[:, t, P * k:P * k + P] for k in range(2) for t in range(TT)], yT_mm)

                    def y_tile(ring_at):
                        return lambda k, t: (yT_hi[:, ring_at, k, P * t:P * t + P],
                                             yT_lo[:, ring_at, k, P * t:P * t + P])

                    pe.wait_ge(xn_dve, 1)
                    pe.wait_ge(xn_act, 1)
                    x_transposes(0)
                    pe.wait_ge(layer_loaded, 16 * 5 * (l + 1))
                    pe.wait_ge(xT_lo, 4)
                    transposes([ps[:, 4, P * g:P * g + P] for g in range(NG)], [ws[:, g, :] for g in range(NG)],
                               ws_T)
                    in_unit(0, 0)
                    in_unit(1, 0)
                    in_unit(2, 1)
                    in_unit(3, 1)
                    pe.wait_ge(rot_i, 2)
                    transposes([ps[:, 5, T * k + P * t:T * k + P * t + P] for k in range(2) for t in range(TT)],
                               [idx[:, t, P * k:P * k + P] for k in range(2) for t in range(TT)], idx_T)
                    in_unit(4, 2, "transposed")
                    in_unit(5, 2, "transposed")
                    pe.wait_ge(idx_out, 1)
                    pe.wait_ge(ws_ready, 1)
                    for t, b0 in ((0, 4), (1, 6)):
                        w = P * (t + 1)
                        for h in range(IH):
                            dst = ps[:, 4, P * h:P * h + P] if t == 0 else ps[:, 6 + h // 2,
                                                                             T * (h % 2):T * (h % 2) + T]
                            ins = mm(dst, iqT[:, h, P * t:P * t + P], ikT[:, 0:w], start=True, stop=True,
                                     skip_group_check=True)
                        ins.then_inc(rel_mm, 1)
                    pe.wait_ge(rot_a, 2)
                    pe.wait_ge(rel_out, 1)
                    for m in range(4):
                        for t in range(TT):
                            ins = nc.tensor.transpose(ps[:, 4 + m // 2, T * (m % 2) + P * t:T * (m % 2) + P * t + P],
                                                      qkr[:, t, P * m:P * m + P], ident[:])
                    ins.then_inc(qk_T, 1)
                    in_unit(6, 3, "mixed")
                    in_unit(7, 3, "mixed")
                    pe.wait_ge(rel_out, 2)
                    pe.wait_ge(block_out, 3)
                    logits(qkT_c, 0, 6, zc_mm)
                    in_unit(8, 4, "transposed")
                    in_unit(9, 4, "transposed")
                    pe.wait_ge(qk_out, 1)
                    logits(qkT_c, 1, 4, zc_mm)
                    in_unit(10, 5)
                    in_unit(11, 5)

                    pe.wait_ge(yT_lo_out, 1)
                    wide_unit(12, 6, y_tile(0), True, True)
                    pe.wait_ge(zexp, 1)
                    pe.wait_ge(zc_out, 1)
                    p_transposes(zc, 0, 6)
                    in_unit(13, 8)
                    pe.wait_ge(pT_out, 1)
                    pv(vc, 0, 7)
                    in_unit(14, 8)
                    pe.wait_ge(zexp, 2)
                    p_transposes(zc, 1, 4)
                    pe.wait_ge(vn_done, 1)
                    for g in range(NG):
                        ins = mm(ps[:, 6, P * g:P * g + P], wsT[:, g, :], vn[:, :, HD * g:HD * g + HD],
                                 start=(g == 0), stop=True, skip_group_check=True)
                    ins.then_inc(sgu_mm, 1)
                    in_unit(15, 9)
                    pe.wait_ge(pT_out, 2)
                    pe.wait_ge(y_out, 1)
                    pv(vc, 1, 7)
                    in_unit(16, 9)
                    pe.wait_ge(yb_done, 1)
                    y_transposes(y_ab, 4)
                    pe.wait_ge(y_out, 2)
                    y_transposes(y_c, 5)
                    pe.wait_ge(yT_lo_out, 2)
                    wide_unit(17, 10, y_tile(1), True, True)
                    pe.wait_ge(yT_lo_out, 3)
                    logits(qkT_a, 0, 4, la_mm)
                    in_unit(18, 12)
                    logits(qkT_a, 1, 6, la_mm)
                    in_unit(19, 12)
                    in_unit(20, 13)
                    pe.wait_ge(la_exp, 1)
                    p_transposes(sc, 0, 4)
                    in_unit(21, 13)
                    pe.wait_ge(pT_out, 3)
                    pv(vi, 0, 5)
                    pe.wait_ge(la_exp, 2)
                    p_transposes(zc, 1, 6)
                    wide_unit(22, 14, y_tile(0), True, True)
                    in_unit(23, 16)
                    pe.wait_ge(pT_out, 4)
                    pe.wait_ge(y_out, 3)
                    pv(vi, 1, 5)
                    in_unit(24, 16)
                    pe.wait_ge(y_out, 4)
                    y_transposes(y_ab, 4)
                    in_unit(25, 17)
                    in_unit(26, 17)
                    pe.wait_ge(yT_lo_out, 4)
                    wide_unit(27, 18, y_tile(1), True, True)
                    in_unit(28, 20)
                    in_unit(29, 20)
                    in_unit(30, 21)
                    pe.wait_ge(gate_sum, 5)

                    def m_transposes(c0):
                        for b in range(2):
                            transposes([ps[:, 4 + c0 // 2 + b, T * k + P * t:T * k + P * t + P]
                                        for k in range(2) for t in range(TT)],
                                       [merged[:, t, P * (c0 + 2 * b + k):P * (c0 + 2 * b + k) + P]
                                        for k in range(2) for t in range(TT)], xT_mm)

                    m_transposes(0)
                    in_unit(31, 21)
                    pe.wait_ge(xT_lo, 6)

                    def m_tile(u):
                        if u < 2:
                            return lambda k, t: (yT_hi[:, u, k, P * t:P * t + P], yT_lo[:, u, k, P * t:P * t + P])
                        return lambda k, t: h_tile(2 * u + k, t)

                    wide_unit(32, 22, m_tile(0), True, False)
                    pe.wait_ge(gate_sum, 6)
                    m_transposes(4)
                    wide_unit(33, 22, m_tile(1), False, False)
                    pe.wait_ge(xT_lo, 8)
                    wide_unit(34, 22, m_tile(2), False, False)
                    wide_unit(35, 22, m_tile(3), False, True)

                    pe.wait_ge(xn_dve, 2)
                    pe.wait_ge(xn_act, 2)
                    x_transposes(8)
                    pe.wait_ge(xT_lo, 12)
                    pe.wait_ge(wr_lo_out, 1)
                    for t in range(TT):
                        for c in range(C):
                            ins = three(ps[:, 0, 36 * t:36 * t + 36], h_tile(c, t), (wr_hi[:, c, :], wr_lo[:, c, :]),
                                        t == 0 and c == 0, c == C - 1)
                    ins.then_inc(route_mm, 1)
                    pe.wait_ge(member_ok, 1)
                    mm(ps[:, 1, 0:32], strict_T[:], member[:, 0, :], start=True, stop=True, skip_group_check=True)
                    mm(ps[:, 1, 32:64], strict_T[:], member[:, 1, :], start=False, stop=False,
                       skip_group_check=True)
                    mm(ps[:, 1, 32:64], ones[:], member[:, 0, :], start=False, stop=True, skip_group_check=True)
                    mm(ps[:, 1, 64:96], ones[:], member[:, 0, :], start=False, stop=False, skip_group_check=True)
                    mm(ps[:, 1, 64:96], ones[:], member[:, 1, :], start=False, stop=True, skip_group_check=True)\
                        .then_inc(rank_mm, 1)
                    pe.wait_ge(passes_ok, 1)
                    pe.wait_ge(xs_lo, 1)

                    passes = pe.alloc_register("pe_passes")
                    pe.reg_mov(passes, 0)

                    def expert_pass(main, g):
                        n = pe.snap(passes)
                        pe.wait_ge(pick_ok, n + 1)
                        for b in range(2):
                            for c in range(4):
                                cc = 4 * b + c
                                for t in range(TT):
                                    for part in (xn_hi, xn_lo):
                                        ins = mm(ps[:, b, P * c:P * c + P], part[:, t, P * cc:P * cc + P],
                                                 pick[:, t, :], start=(t == 0 and part is xn_hi),
                                                 stop=(t == 1 and part is xn_lo), skip_group_check=True)
                            ins.then_inc(gath_mm, 1)
                        pe.wait_ge(wpick_ok, n + 1)
                        pe.wait_ge(x_add, 4 * n + 1)
                        for t in range(TT):
                            ins = nc.tensor.transpose(ps[:, 4, P * t:P * t + P], wpick[:, t, :], ident[:])
                        ins.then_inc(scat_T, 1)

                        def gate_up(i):
                            if i == 0:
                                pe.wait_ge(gath_out, 2 * n + 2)
                            for part in range(2):
                                arrived(3 * i + part)
                            w = ring[:, 3 * i * UNIT:(3 * i + 2) * UNIT]\
                                .rearrange("p (s c f) -> p s c f", s=2, c=C)
                            for c in range(C):
                                for j in range(4):
                                    ins = mm(ps[32 * j:32 * j + 32, 2 + i % 2, 0:P],
                                             hG[:, c, SLOTS * i:SLOTS * i + SLOTS], w[:, :, c, 64 * j:64 * j + 64],
                                             start=(c == 0), stop=(c == C - 1))
                            ins.then_inc(gu_mm, 1)

                        def arrived(s):
                            k = (LOADS_LOW * l + NU // MRING) if s < MRING else LOADS_HIGH * l
                            pe.wait_ge(ring_loaded[s], 16 * (k + g + 1))

                        def hidden(i):
                            pe.wait_ge(hid_out, 4 * n + i + 1)
                            if i == 0:
                                pe.wait_ge(scat_T_out, n + 1)
                            for k in range(2):
                                ins = mm(ps[:, 4, SLOTS * k:SLOTS * k + SLOTS], hid[:, i % 2, k::2],
                                         ident[0:SLOTS, 0:SLOTS], start=True, stop=True)
                            ins.then_inc(hid_T, 1)

                        def down(i):
                            arrived(3 * i + 2)
                            pe.wait_ge(hidT_out, 4 * n + i + 1)
                            if i >= 2:
                                pe.wait_ge(y_act, 4 * n + i - 1)
                                pe.wait_ge(y_dve, 4 * n + i - 1)
                            w = slot(3 * i + 2).rearrange("p (k d) -> p k d", k=2)
                            for k in range(2):
                                for q in range(4):
                                    ins = mm(ps[32 * q:32 * q + 32, 5 + i % 2, 0:256], hidT[:, i % 2, k, :],
                                             w[:, k, 256 * q:256 * q + 256], start=(k == 0), stop=(k == 1))
                            ins.then_inc(down_mm, 1)

                        gate_up(0)
                        gate_up(1)
                        for i in range(GE):
                            hidden(i)
                            down(i)
                            if i + 2 < GE:
                                gate_up(i + 2)
                            if main:
                                pe.wait_ge(down_mm, 4 * n + i + 1)
                                pe.sem_inc(unit_used, 3)
                        pe.wait_ge(y_act, 4 * n + 4)
                        pe.wait_ge(y_dve, 4 * n + 4)
                        for k in range(4):
                            t, hf = k // 2, k % 2
                            if k >= 2:
                                pe.wait_ge(x_add, 4 * n + k)
                            mm(ps[:, (7, 4)[hf], :], scatT[:, t, :], y_slots[:, 512 * hf:512 * hf + 512],
                               start=True, stop=True).then_inc(scat_mm, 1)
                        pe.reg_add(passes, passes, 1)

                    with pe.Fori(0, GROUPS) as g:
                        p_ = pe.value_load(npass[0:1, bass.ds(g, 1)], min_val=1, max_val=MAXPASS)
                        with pe.If(p_ > 1):
                            with pe.Fori(1, p_):
                                expert_pass(False, g)
                        expert_pass(True, g)

                @layer.scalar
                def _(act):
                    A = nc.scalar.activation

                    def hi(u):
                        s = u % MRING
                        act.wait_ge(ring_loaded[s], 16 * (LOADS_LOW * l + u // MRING + 1))
                        for v in (2 * u, 2 * u + 1):
                            if v >= SPLITS:
                                act.wait_ge(half_used, v - SPLITS + 1)
                            A(half_view(split_hi[:, v % SPLITS, :], v), raw_half(v), ACT.Copy).then_inc(hi_done, 1)

                    def block_evac(k, dst, b0, func=ACT.Copy, n=512):
                        act.wait_ge(half_used, 2 * LAST_UNIT[k] + 2)
                        A(dst, ps[:, b0:b0 + 2, 0:n], func).then_inc(block_out, 1)

                    def squares_of_x():
                        for t in range(TT):
                            A(wide[:, t, :], x[:, t, :], ACT.Square, accum_out=ss[:, t:t + 1]).then_inc(squares, 1)

                    def normalise(k):
                        act.wait_ge(var_ready, k)
                        A(sd, var, ACT.Sqrt).then_inc(root, 1)
                        act.wait_ge(inv_rms, k)
                        act.wait_ge(squares, 2 * k)
                        A(xnp[1], xp[1], ACT.Copy, scale=ir[:, 1:2]).then_inc(xn_act, 1)

                    def xT_hi_parts(k, g0):
                        act.wait_ge(small_ready, 1)
                        for b in range(4):
                            act.wait_ge(xT_mm, k + b + 1)
                            for j in range(2):
                                c = 2 * b + j
                                ins = A(hT_hi[:, c, :], ps[:, 4 + b, T * j:T * j + T], ACT.Copy,
                                        scale=small[:, g0 + c:g0 + c + 1])
                            ins.then_inc(xT_hi, 1)

                    def yT_high(k, at, b0):
                        act.wait_ge(yT_mm, k)
                        A(yT_hi[:, at, :, :], ps[:, b0, :], ACT.Copy).then_inc(yT_hi_out, 1)

                    def p_evac(k, t, b0):
                        act.wait_ge(pT_mm, k)
                        A(pT[:, 0:t + 1, :, :], ps[:, b0:b0 + t + 1, :].rearrange("p b (h q) -> p b h q", h=NH),
                          ACT.Copy).then_inc(pT_out, 1)

                    def softplus(t):
                        w = P * (t + 1)
                        z, s_ = zc[:, :, 0:w], sc[:, :, 0:w]
                        act.wait_ge(zc_out, t + 1)
                        A(s_, z, ACT.Abs).then_inc(zabs, 1)
                        act.wait_ge(zabs, 2 * t + 1)
                        A(s_, s_, ACT.Exp, scale=-1.0).then_inc(zabs, 1)
                        act.wait_ge(zabs, 2 * t + 2)
                        A(s_, s_, ACT.Ln, bias=1.0).then_inc(zln, 1)

                    def stick_exp(t):
                        w = P * (t + 1)
                        act.wait_ge(zarg, t + 1)
                        A(zc[:, :, 0:w], zc[:, :, 0:w], ACT.Exp).then_inc(zexp, 1)

                    def softmax_exp(t, buf):
                        w = P * (t + 1)
                        act.wait_ge(la_max, t + 1)
                        for s_ in range(NH):
                            ins = A(buf[:, s_, 0:w], buf[:, s_, 0:w], ACT.Exp, bias=lneg[:, s_:s_ + 1],
                                    scale=ATT_SCALE, accum_out=lsum[:, s_:s_ + 1])
                        ins.then_inc(la_exp, 1)

                    hi_first = hi
                    hi_first(0)
                    squares_of_x()
                    normalise(1)
                    xT_hi_parts(0, PG1)
                    hi(1)
                    hi(2)
                    block_evac(0, vi[:, :, :], 0, n=420)
                    hi(3)
                    hi(4)
                    block_evac(1, uv[:, :, :], 2)
                    hi(5)
                    act.wait_ge(idx_T, 1)
                    act.wait_ge(first, 1)
                    for h in range(IH):
                        A(iqT[ID * h:ID * h + ID, h, :], ps[ID * h:ID * h + ID, 5, 0:T], ACT.Copy)
                    A(ikT, ps[:, 5, T:2 * T], ACT.Copy).then_inc(idx_out, 1)
                    hi(6)
                    block_evac(2, qkT_c.rearrange("p m t -> p (m t)").rearrange("p (a n) -> p a n", a=2), 0)
                    act.wait_ge(rel_mm, 1)
                    A(zc[:, 0:2, :], ps[:, 4, :], ACT.Relu).then_inc(rel_out, 1)
                    act.wait_ge(rel_mm, 2)
                    A(sc[:, :, :], ps[:, 6:8, :], ACT.Relu).then_inc(rel_out, 1)
                    hi(7)
                    act.wait_ge(qk_T, 1)
                    A(qkT_a, ps[:, 4:6, :], ACT.Copy).then_inc(qk_out, 1)
                    hi(8)
                    act.wait_ge(half_used, 2 * LAST_UNIT[3] + 2)
                    A(vc[:, :, :], ps[:, 2, :], ACT.Copy)
                    A(bdT, ps[:, 3, :], ACT.Copy).then_inc(block_out, 1)
                    hi(9)
                    softplus(0)
                    hi(10)
                    block_evac(4, cxT.rearrange("p m t -> p (m t)").rearrange("p (a n) -> p a n", a=2), 0)
                    hi(11)
                    act.wait_ge(conv_y, 1)
                    A(yT_hi[:, 0, :, :], cxT[:, 2:4, :], ACT.Copy).then_inc(yT_hi_out, 1)
                    stick_exp(0)
                    hi(12)
                    block_evac(5, uv[:, :, :], 2, ACT.Gelu_apprx_tanh)
                    hi(13)
                    block_evac(6, br[:, 0, :, :], 0)
                    block_evac(7, br[:, 1, :, :], 2)
                    act.wait_ge(ln_var, 1)
                    A(lsd, lvar, ACT.Sqrt).then_inc(ln_root, 1)
                    hi(14)
                    p_evac(1, 0, 6)
                    softplus(1)
                    hi(15)
                    stick_exp(1)
                    block_evac(8, sig[:, :, :], 0, ACT.Sigmoid)
                    hi(16)
                    p_evac(2, 1, 4)
                    hi(17)
                    yT_high(1, 1, 4)
                    yT_high(2, 0, 5)
                    act.wait_ge(gate_prod, 1)
                    block_evac(9, sig[:, :, :], 2, ACT.Sigmoid)
                    hi(18)
                    act.wait_ge(gate_prod, 2)
                    block_evac(10, br[:, 0, :, :], 0)
                    block_evac(11, br[:, 1, :, :], 2)
                    hi(19)
                    hi(20)
                    softmax_exp(0, sc)
                    block_evac(12, sig[:, :, :], 0, ACT.Sigmoid)
                    hi(21)
                    softmax_exp(1, zc)
                    hi(22)
                    p_evac(3, 0, 4)
                    act.wait_ge(gate_sum, 1)
                    block_evac(13, sig[:, :, :], 2, ACT.Sigmoid)
                    hi(23)
                    act.wait_ge(pv_mm, 3)
                    p_evac(4, 1, 6)
                    act.wait_ge(gate_prod, 4)
                    block_evac(14, br[:, 0, :, :], 0)
                    block_evac(15, br[:, 1, :, :], 2)
                    hi(24)
                    hi(25)
                    act.wait_ge(gate_sum, 2)
                    block_evac(16, sig[:, :, :], 0, ACT.Sigmoid)
                    hi(26)
                    yT_high(3, 1, 4)
                    hi(27)
                    act.wait_ge(gate_sum, 3)
                    block_evac(17, sig[:, :, :], 2, ACT.Sigmoid)
                    hi(28)
                    act.wait_ge(gate_prod, 6)
                    block_evac(18, br[:, 0, :, :], 0)
                    block_evac(19, br[:, 1, :, :], 2)
                    hi(29)
                    hi(30)
                    act.wait_ge(gate_sum, 4)
                    block_evac(20, sig[:, :, :], 0, ACT.Sigmoid)
                    hi(31)

                    def mT_high(k, dst, b0):
                        for b in range(2):
                            act.wait_ge(xT_mm, k + b + 1)
                            A(dst(b), ps[:, b0 + b, :], ACT.Copy).then_inc(xT_hi, 1)

                    mT_high(4, lambda b: yT_hi[:, b, :, :], 4)
                    hi(32)
                    act.wait_ge(gate_sum, 5)
                    block_evac(21, sig[:, :, :], 2, ACT.Sigmoid)
                    hi(33)
                    mT_high(6, lambda b: hT_hi[:, 4 + 2 * b:6 + 2 * b, :], 6)
                    hi(34)
                    hi(35)

                    act.wait_ge(x_mid, 2)
                    squares_of_x()
                    normalise(2)
                    act.wait_ge(xn_dve, 2)
                    act.wait_ge(half_used, 2 * NU)
                    act.wait_ge(layer_loaded, 16 * 5 * (l + 1))
                    A(wr_hi, wr[:], ACT.Copy).then_inc(wr_hi_out, 1)
                    xT_hi_parts(8, PG2)
                    act.wait_ge(xn_act, 2)
                    A(xn_hi, wide[:], ACT.Copy).then_inc(xs_hi, 1)
                    act.wait_ge(gmax, 1)
                    A(rt[:, 0:8], rt[:, 8:16], ACT.Exp).then_inc(gexp, 1)
                    act.wait_ge(emax, 1)
                    A(rt[:, 16:18], rt[:, 18:20], ACT.Exp).then_inc(eexp, 1)
                    act.wait_ge(passes_ok, 1)

                    passes = act.alloc_register("act_passes")
                    act.reg_mov(passes, 0)

                    def expert_pass():
                        n = act.snap(passes)
                        act.wait_ge(scat_T, n + 1)
                        A(scatT, ps[:, 4, 0:2 * P], ACT.Copy).then_inc(scat_T_out, 1)

                        def silu_of(i):
                            act.wait_ge(gu_mm, 4 * n + i + 1)
                            A(silu[:, i % 2, :], ps[:, 2 + i % 2, 0:64], ACT.Silu).then_inc(silu_out, 1)

                        silu_of(0)
                        silu_of(1)
                        for i in range(GE):
                            act.wait_ge(hid_T, 4 * n + i + 1)
                            A(hidT[:, i % 2, :, :], ps[:, 4, 0:2 * SLOTS], ACT.Copy).then_inc(hidT_out, 1)
                            act.wait_ge(down_mm, 4 * n + i + 1)
                            for q in range(2):
                                ins = A(y_slots[SLOTS * i:SLOTS * i + SLOTS, 256 * q:256 * q + 256],
                                        ps[32 * q:32 * q + 32, 5 + i % 2, 0:256], ACT.Copy)
                            ins.then_inc(y_act, 1)
                            if i + 2 < GE:
                                silu_of(i + 2)
                        act.reg_add(passes, passes, 1)

                    with act.Fori(0, GROUPS) as g:
                        p_ = act.value_load(npass[0:1, bass.ds(g, 1)], min_val=1, max_val=MAXPASS)
                        with act.If(p_ > 1):
                            with act.Fori(1, p_):
                                expert_pass()
                        expert_pass()

                @layer.vector
                def _(dve):
                    V = nc.vector
                    n = [0]

                    def link(ins):
                        n[0] += 1
                        ins.then_inc(dve_c, 1)
                        dve.wait_ge(dve_c, n[0])

                    def lo(u):
                        for v in (2 * u, 2 * u + 1):
                            dve.wait_ge(hi_done, v + 1)
                            V.tensor_tensor(half_view(split_lo[:, v % SPLITS, :], v), raw_half(v),
                                            half_view(split_hi[:, v % SPLITS, :], v).bitcast(F32),
                                            ALU.subtract).then_inc(lo_done, 1)

                    def norm(k):
                        dve.wait_ge(squares, 2 * k)
                        link(V.tensor_scalar(var, ss, 1.0 / D, EPS, ALU.mult, ALU.add))
                        V.tensor_scalar(nt, var, -0.5, None, ALU.mult).then_inc(var_ready, 1)
                        dve.wait_ge(root, k)
                        newton(ir, sd, nt).then_inc(inv_rms, 1)
                        dve.wait_ge(inv_rms, k)
                        V.tensor_scalar(xnp[0], xp[0], ir[:, 0:1], None, ALU.mult).then_inc(xn_dve, 1)

                    def newton(r, s_, mhalf_v):
                        link(V.reciprocal(r, s_))
                        link(V.tensor_tensor(scal[:, 60:62], r, r, ALU.mult))
                        link(V.tensor_tensor(scal[:, 60:62], scal[:, 60:62], mhalf_v, ALU.mult))
                        link(V.tensor_scalar(scal[:, 60:62], scal[:, 60:62], 1.5, None, ALU.add))
                        return V.tensor_tensor(r, r, scal[:, 60:62], ALU.mult)

                    def xT_lo_parts(k, g0):
                        for b in range(4):
                            dve.wait_ge(xT_hi, k + b + 1)
                            for j in range(2):
                                c = 2 * b + j
                                ins = V.scalar_tensor_tensor(hT_lo[:, c, :], ps[:, 4 + b, T * j:T * j + T],
                                                             small[:, g0 + c:g0 + c + 1],
                                                             hT_hi[:, c, :].bitcast(F32), ALU.mult, ALU.subtract)
                            ins.then_inc(xT_lo, 1)

                    def yT_low(k, at, b0):
                        dve.wait_ge(yT_hi_out, k)
                        V.tensor_tensor(yT_lo[:, at, :, :].rearrange("p k t -> p (k t)"), ps[:, b0, :],
                                        yT_hi[:, at, :, :].rearrange("p k t -> p (k t)").bitcast(F32),
                                        ALU.subtract).then_inc(yT_lo_out, 1)

                    def index_score(t):
                        w = P * (t + 1)
                        dve.wait_ge(rel_out, t + 1)
                        for h in range(IH):
                            rel = zc[:, 0:2, :].rearrange("p a s -> p (a s)")[:, P * h:P * h + P] if t == 0 \
                                else sc[:, h, :]
                            prev = (mask_a[:, P:] if t == 0 else mask_a[:]) if h == 0 else score[:, 0:w]
                            link(V.scalar_tensor_tensor(score[:, 0:w], rel, vi[:, t, 416 + h:417 + h], prev,
                                                        ALU.mult, ALU.add))

                    def top_rounds(t, rounds):
                        w = P * (t + 1)
                        for _ in range(rounds):
                            link(V.max(top8, score[:, 0:w]))
                            link(V.match_replace(score[:, 0:w], top8, score[:, 0:w], TAKEN))

                    def select_mask(t):
                        w = P * (t + 1)
                        dst = mb[:, 0:P] if t == 0 else mb[:, P:]
                        link(V.tensor_scalar(dst, score[:, 0:w], TAKEN / 1.5, MASKED, ALU.is_gt, ALU.mult))
                        link(V.tensor_tensor(dst, dst, mask_a[:, P:] if t == 0 else mask_a[:], ALU.add))

                    def stick_logits(t, b0):
                        w = P * (t + 1)
                        m = mask_c[:, P:] if t == 0 else mask_c[:]
                        dve.wait_ge(zc_mm, t + 1)
                        if t == 1:
                            dve.wait_ge(pT_mm, 1)
                        V.scalar_tensor_tensor(zc[:, :, 0:w],
                                               ps[:, b0:b0 + 2, :].rearrange("p b n -> p (b n)")
                                               .rearrange("p (h s) -> p h s", h=NH)[:, :, 0:w],
                                               ATT_SCALE, m.rearrange("p (o s) -> p o s", o=1)
                                               .broadcast_to([P, NH, w]), ALU.mult, ALU.add).then_inc(zc_out, 1)

                    def stick_weights(t):
                        w = P * (t + 1)
                        z, s_ = zc[:, :, 0:w], sc[:, :, 0:w]
                        dve.wait_ge(zln, t + 1)
                        link(V.scalar_tensor_tensor(s_, z, 0.0, s_, ALU.max, ALU.add))
                        for h in range(NH):
                            rev = sc[:, h, 0:w][:, ::-1]
                            ones_w = ones[:, 0:1].broadcast_to([P, w])
                            ins = V.tensor_tensor_scan(rev, ones_w, rev, 0.0, ALU.mult, ALU.add)
                        link(ins)
                        V.tensor_tensor(z, z, s_, ALU.subtract).then_inc(zarg, 1)

                    def conv():
                        dve.wait_ge(block_out, 5)
                        link(V.tensor_tensor(cxT[:, 0:2, :], cxT[:, 0:2, :], cxT[:, 2:4, :], ALU.mult))
                        for k in range(2):
                            w_ = small[:, PCW + 3 * k:PCW + 3 * k + 3]
                            z, y = cxT[:, k, :], cxT[:, 2 + k, :]
                            link(V.tensor_scalar(y, z, w_[:, 2:3], None, ALU.mult))
                            link(V.scalar_tensor_tensor(y[:, 1:T], z[:, 0:T - 1], w_[:, 1:2], y[:, 1:T],
                                                        ALU.mult, ALU.add))
                            link(V.scalar_tensor_tensor(y[:, 2:T], z[:, 0:T - 2], w_[:, 0:1], y[:, 2:T],
                                                        ALU.mult, ALU.add))
                        V.tensor_tensor(cxT[:, 2:4, :], cxT[:, 2:4, :], bdT, ALU.mult).then_inc(conv_y, 1)
                        dve.wait_ge(conv_y, 1)
                        dve.wait_ge(yT_hi_out, 1)
                        V.tensor_tensor(yT_lo[:, 0, :, :], cxT[:, 2:4, :], yT_hi[:, 0, :, :].bitcast(F32),
                                        ALU.subtract).then_inc(yT_lo_out, 1)

                    def ln_stats():
                        dve.wait_ge(block_out, 6)
                        for t in range(TT):
                            link(V.bn_stats(bn[:, t, :], uv[:, t, BW:]))
                            link(V.bn_aggr(lmv[:, t, :], bn[:, t, :]))
                        link(V.tensor_scalar(lvar, lmv[:, :, 1], EPS, None, ALU.add))
                        V.tensor_scalar(lrs, lvar, -0.5, None, ALU.mult).then_inc(ln_var, 1)

                    def ln_apply():
                        dve.wait_ge(ln_root, 1)
                        dve.wait_ge(ln_var, 1)
                        link(newton(lsd, lsd, lrs))
                        for t in range(TT):
                            ins = V.tensor_scalar(vn[:, t, :], uv[:, t, BW:], lmv[:, t, 0:1], lsd[:, t:t + 1],
                                                  ALU.subtract, ALU.mult)
                        ins.then_inc(vn_dve, 1)

                    def sgu_gate():
                        dve.wait_ge(sgu_mm, 1)
                        for g in range(NG):
                            cols = slice(HD * g, HD * g + HD)
                            ins = V.scalar_tensor_tensor(y_ab[:, :, cols],
                                                         ps[:, 6, P * g:P * g + P].rearrange("p (t f) -> p t f", t=TT),
                                                         small[:, PBS + g:PBS + g + 1], uv[:, :, cols],
                                                         ALU.add, ALU.mult)
                        ins.then_inc(yb_done, 1)

                    def y_evac_c(t):
                        dve.wait_ge(pv_mm, t + 1)
                        V.tensor_copy(y_c[:, t, :], ps[:, 7, 0:BW]).then_inc(y_out, 1)

                    def sparse_logits(t, b0, buf):
                        w = P * (t + 1)
                        m = mb[:, 0:P] if t == 0 else mb[:, P:]
                        dve.wait_ge(la_mm, t + 1)
                        link(V.tensor_tensor(buf[:, :, 0:w],
                                             ps[:, b0:b0 + 2, :].rearrange("p b n -> p (b n)")
                                             .rearrange("p (h s) -> p h s", h=NH)[:, :, 0:w],
                                             m.rearrange("p (o s) -> p o s", o=1).broadcast_to([P, NH, w]),
                                             ALU.add))
                        link(V.tensor_reduce(lmax, buf[:, :, 0:w], AX.X, ALU.max))
                        if t == 1:
                            dve.wait_ge(la_exp, 1)
                            link(V.reciprocal(scal[:, 52:56], lsum))
                        V.tensor_scalar(lneg, lmax, -ATT_SCALE, None, ALU.mult).then_inc(la_max, 1)

                    def y_evac_a(t):
                        dve.wait_ge(pv_mm, t + 3)
                        inv = scal[:, 52:56]
                        if t == 1:
                            dve.wait_ge(y_out, 3)
                            link(V.reciprocal(inv, lsum))
                        for r in range(2):
                            ins = V.tensor_tensor(
                                y_ab[:, t, :].rearrange("p (m r f) -> p r m f", m=2, r=2)[:, r],
                                ps[:, 5, 0:BW].rearrange("p (m r f) -> p r m f", m=2, r=2)[:, r],
                                inv[:, 2 * r:2 * r + 2].rearrange("p (m o) -> p m o", o=1)
                                .broadcast_to([P, 2, HD]), ALU.mult)
                        ins.then_inc(y_out, 1)

                    def gate(j, use):
                        hf = j % 2
                        dve.wait_ge(block_out, use + 1)
                        dst = merged[:, :, 512 * hf:512 * hf + 512] if j < 2 else sig[:]
                        V.tensor_tensor(dst, sig[:], br[:, hf, :, :], ALU.mult).then_inc(gate_prod, 1)

                    def mT_low(k, dst, hi_part, b0):
                        for b in range(2):
                            dve.wait_ge(xT_hi, k + b + 1)
                            V.tensor_tensor(dst(b), ps[:, b0 + b, :].rearrange("p (k t) -> p k t", k=2),
                                            hi_part(b).bitcast(F32), ALU.subtract).then_inc(xT_lo, 1)

                    V.tensor_copy(small[:], small_all[:, bass.ds(l, 1), :].rearrange("p o n -> p (o n)"))\
                        .then_inc(small_ready, 1)
                    lo(0)
                    norm(1)
                    dve.wait_ge(small_ready, 1)
                    xT_lo_parts(0, PG1)
                    lo(1)
                    dve.wait_ge(ws_T, 1)
                    V.tensor_tensor(wsT[:], bank(4).rearrange("p (g t) -> p g t", g=NG),
                                    incl_T[:].rearrange("p (o t) -> p o t", o=1).broadcast_to([P, NG, P]),
                                    ALU.mult).then_inc(ws_ready, 1)
                    for u in range(2, 7):
                        lo(u)
                    index_score(0)
                    lo(7)
                    top_rounds(0, TOPK // 8)
                    select_mask(0)
                    lo(8)
                    index_score(1)
                    top_rounds(1, 4)
                    lo(9)
                    stick_logits(0, 6)
                    top_rounds(1, TOPK // 8 - 4)
                    select_mask(1)
                    lo(10)
                    stick_weights(0)
                    lo(11)
                    conv()
                    lo(12)
                    lo(13)
                    ln_stats()
                    stick_logits(1, 4)
                    lo(14)
                    ln_apply()
                    stick_weights(1)
                    lo(15)
                    y_evac_c(0)
                    gate(0, 8)
                    lo(16)
                    sgu_gate()
                    lo(17)
                    y_evac_c(1)
                    yT_low(2, 1, 4)
                    yT_low(3, 0, 5)
                    gate(1, 9)
                    lo(18)
                    lo(19)
                    sparse_logits(0, 4, sc)
                    lo(20)
                    sparse_logits(1, 6, zc)
                    gate(2, 12)
                    lo(21)
                    lo(22)
                    y_evac_a(0)
                    gate(3, 13)
                    lo(23)
                    lo(24)
                    lo(25)
                    y_evac_a(1)
                    gate(4, 16)
                    lo(26)
                    yT_low(4, 1, 4)
                    lo(27)
                    gate(5, 17)
                    lo(28)
                    lo(29)
                    lo(30)
                    gate(6, 20)
                    lo(31)
                    mT_low(4, lambda b: yT_lo[:, b, :, :], lambda b: yT_hi[:, b, :, :], 4)
                    lo(32)
                    gate(7, 21)
                    dve.wait_ge(gate_prod, 8)
                    m_ = merged[:, :, 512:1024]
                    V.tensor_tensor(m_, m_, sig[:], ALU.add).then_inc(gate_sum, 1)
                    lo(33)
                    mT_low(6, lambda b: hT_lo[:, 4 + 2 * b:6 + 2 * b, :], lambda b: hT_hi[:, 4 + 2 * b:6 + 2 * b, :], 6)
                    lo(34)
                    lo(35)
                    dve.wait_ge(half_used, 2 * NU)
                    for hf in range(2):
                        xs = x[:, :, 512 * hf:512 * hf + 512]
                        V.tensor_tensor(xs, xs, ps[:, 2 * hf:2 * hf + 2, :], ALU.add).then_inc(x_mid, 1)

                    norm(2)
                    dve.wait_ge(wr_hi_out, 1)
                    V.tensor_tensor(wr_lo, wr[:], wr_hi.bitcast(F32), ALU.subtract).then_inc(wr_lo_out, 1)
                    xT_lo_parts(8, PG2)
                    dve.wait_ge(route_mm, 1)
                    bias = small[:, PBR:PBR + NG + NE].rearrange("p (o e) -> p o e", o=1)\
                        .broadcast_to([P, TT, NG + NE])
                    link(V.tensor_tensor(rl, ps[:, 0, 0:TT * 36].rearrange("p (t e) -> p t e", t=TT), bias, ALU.add))

                    def r2(k):
                        return rt[:, k:k + 2]

                    def r3(k, w):
                        return rt[:, k:k + 2 * w].rearrange("p (t e) -> p t e", t=TT)

                    def bc(ap, w):
                        return ap.rearrange("p (t o) -> p t o", o=1).broadcast_to([P, TT, w])

                    def first_of(dst, eq, w):
                        dsc = desc[:, EG - w:].rearrange("p (o e) -> p o e", o=1).broadcast_to([P, TT, w])
                        link(V.tensor_tensor(eq, eq, dsc, ALU.mult))
                        link(V.tensor_reduce(r2(100), eq, AX.X, ALU.max))
                        link(V.tensor_tensor(dst, eq, bc(r2(100), w), ALU.is_equal))

                    g_logit = rl[:, :, 0:NG]
                    link(V.tensor_reduce(r2(102), g_logit, AX.X, ALU.max))
                    link(V.tensor_tensor(r3(32, NG), g_logit, bc(r2(102), NG), ALU.is_ge))
                    V.tensor_tensor(r3(8, NG), g_logit, bc(r2(102), NG), ALU.subtract).then_inc(gmax, 1)
                    first_of(r3(40, NG), r3(32, NG), NG)
                    sel = r3(40, NG).rearrange("p t (g o) -> p t g o", o=1).broadcast_to([P, TT, NG, EG])
                    link(V.tensor_tensor(prod32, rl[:, :, NG:].rearrange("p t (g e) -> p t g e", g=NG), sel,
                                         ALU.mult))
                    link(V.tensor_reduce(r3(48, EG), prod32.rearrange("p t g e -> p t e g"), AX.X, ALU.add))
                    ing = r3(48, EG)
                    link(V.tensor_reduce(r2(104), ing, AX.X, ALU.max))
                    link(V.tensor_tensor(r3(64, EG), ing, bc(r2(104), EG), ALU.is_ge))
                    first_of(r3(80, EG), r3(64, EG), EG)
                    link(V.scalar_tensor_tensor(ing, r3(80, EG), -3.0e38, ing, ALU.mult, ALU.add))
                    link(V.tensor_reduce(r2(106), ing, AX.X, ALU.max))
                    link(V.tensor_tensor(r3(64, EG), ing, bc(r2(106), EG), ALU.is_ge))
                    V.tensor_tensor(r2(18), r2(106), r2(104), ALU.subtract).then_inc(emax, 1)
                    first_of(r3(112, EG), r3(64, EG), EG)
                    link(V.tensor_tensor(r3(64, EG), r3(80, EG), r3(112, EG), ALU.add))
                    m4 = member.rearrange("p t (g e) -> p t g e", g=NG)
                    both = r3(64, EG).rearrange("p t (o e) -> p t o e", o=1).broadcast_to([P, TT, NG, EG])
                    V.tensor_tensor(m4, sel, both, ALU.mult).then_inc(member_ok, 1)
                    dve.wait_ge(gexp, 1)
                    link(V.tensor_reduce(r2(108), r3(0, NG), AX.X, ALU.add))
                    link(V.reciprocal(r2(108), r2(108)))
                    dve.wait_ge(eexp, 1)
                    link(V.tensor_scalar(r2(110), r2(16), 1.0, None, ALU.add))
                    link(V.reciprocal(r2(110), r2(110)))
                    link(V.tensor_tensor(r2(110), r2(110), r2(108), ALU.mult))
                    link(V.tensor_tensor(r2(108), r2(110), r2(16), ALU.mult))
                    link(V.tensor_tensor(r3(80, EG), r3(80, EG), bc(r2(110), EG), ALU.mult))
                    link(V.tensor_tensor(r3(112, EG), r3(112, EG), bc(r2(108), EG), ALU.mult))
                    link(V.tensor_tensor(r3(80, EG), r3(80, EG), r3(112, EG), ALU.add))
                    link(V.tensor_tensor(wt[:].rearrange("p t (g e) -> p t g e", g=NG), sel,
                                         r3(80, EG).rearrange("p t (o e) -> p t o e", o=1)
                                         .broadcast_to([P, TT, NG, EG]), ALU.mult))
                    dve.wait_ge(rank_mm, 1)
                    link(V.tensor_copy(cnts[:, 0:32], ps[:, 1, 64:96]))
                    link(V.scalar_tensor_tensor(rankm[:], ps[:, 1, 0:64].rearrange("p (t e) -> p t e", t=TT), 1.0,
                                                member, ALU.add, ALU.mult))
                    link(V.tensor_scalar(rankm[:], rankm[:], -1.0, None, ALU.add))
                    link(V.tensor_reduce(cnts[:, 32:40], cnts[:, 0:32].rearrange("p (g e) -> p g e", e=GE), AX.X,
                                         ALU.max))
                    over = prod32.rearrange("p t g e -> p (t g e)")[:, 0:GROUPS * (MAXPASS - 1)]\
                        .rearrange("p (g k) -> p g k", g=GROUPS)
                    link(V.tensor_tensor(over, cnts[:, 32:40].rearrange("p (g o) -> p g o", o=1)
                                         .broadcast_to([P, GROUPS, MAXPASS - 1]),
                                         limits[:].rearrange("p (o k) -> p o k", o=1)
                                         .broadcast_to([P, GROUPS, MAXPASS - 1]), ALU.is_gt))
                    link(V.tensor_reduce(cnts[:, 40:48], over, AX.X, ALU.add))
                    link(V.tensor_scalar(cnts[:, 40:48], cnts[:, 40:48], 1.0, None, ALU.add))
                    V.tensor_copy(npass[:], cnts[0:1, 40:48]).then_inc(passes_ok, 1)
                    dve.wait_ge(xs_hi, 1)
                    V.tensor_tensor(xn_lo, wide[:], xn_hi.bitcast(F32), ALU.subtract).then_inc(xs_lo, 1)
                    dve.wait_ge(passes_ok, 1)
                    V.tensor_copy(slot_cur[:], slot_no[:]).then_inc(slot_c, 1)
                    V.memset(scal[:, 59:60], 0.0).then_inc(x_add, 1)

                    passes = dve.alloc_register("dve_passes")
                    dve.reg_mov(passes, 0)

                    def expert_pass(main, g):
                        k_ = dve.snap(passes)
                        places = slot_no
                        if not main:
                            dve.wait_ge(slot_c, dve.snap(writes))
                            V.tensor_scalar(slot_cur[:], slot_cur[:], float(SLOTS), None, ALU.add)\
                                .then_inc(slot_c, 1)
                            dve.reg_add(writes, writes, 1)
                            dve.wait_ge(slot_c, dve.snap(writes))
                            places = slot_cur
                        for t in range(TT):
                            ins = V.tensor_tensor(pick[:, t, :].rearrange("p (i s) -> p i s", i=GE),
                                                  rankm[:, t, bass.ds(g * GE, GE)]
                                                  .rearrange("p (i o) -> p i o", o=1)
                                                  .broadcast_to([P, GE, SLOTS]),
                                                  places[:].rearrange("p (o s) -> p o s", o=1)
                                                  .broadcast_to([P, GE, SLOTS]), ALU.is_equal)
                        ins.then_inc(pick_ok, 1)
                        dve.wait_ge(pick_ok, k_ + 1)
                        for t in range(TT):
                            ins = V.tensor_tensor(wpick[:, t, :].rearrange("p (i s) -> p i s", i=GE),
                                                  pick[:, t, :].rearrange("p (i s) -> p i s", i=GE).bitcast(F32),
                                                  wt[:, t, bass.ds(g * GE, GE)]
                                                  .rearrange("p (i o) -> p i o", o=1)
                                                  .broadcast_to([P, GE, SLOTS]), ALU.mult)
                        ins.then_inc(wpick_ok, 1)
                        for b in range(2):
                            dve.wait_ge(gath_mm, 2 * k_ + b + 1)
                            V.tensor_tensor(hG[:, 4 * b:4 * b + 4, :],
                                            bank(b).rearrange("p (c s) -> p c s", c=4),
                                            small[:, PG2 + 4 * b:PG2 + 4 * b + 4].rearrange("p (c o) -> p c o", o=1)
                                            .broadcast_to([P, 4, P]), ALU.mult).then_inc(gath_out, 1)

                        def hidden(i):
                            dve.wait_ge(silu_out, 4 * k_ + i + 1)
                            for j in range(4):
                                ins = V.tensor_tensor(hid[:, i % 2, 64 * j:64 * j + 64],
                                                      silu[32 * j:32 * j + 32, i % 2, :],
                                                      ps[32 * j:32 * j + 32, 2 + i % 2, 64:128], ALU.mult)
                            ins.then_inc(hid_out, 1)

                        hidden(0)
                        hidden(1)
                        for i in range(GE):
                            dve.wait_ge(down_mm, 4 * k_ + i + 1)
                            for q in (2, 3):
                                ins = V.tensor_copy(y_slots[SLOTS * i:SLOTS * i + SLOTS, 256 * q:256 * q + 256],
                                                    ps[32 * q:32 * q + 32, 5 + i % 2, 0:256])
                            ins.then_inc(y_dve, 1)
                            if i + 2 < GE:
                                hidden(i + 2)
                        for k in range(4):
                            t, hf = k // 2, k % 2
                            dve.wait_ge(scat_mm, 4 * k_ + k + 1)
                            xs = x[:, t, 512 * hf:512 * hf + 512]
                            V.tensor_tensor(xs, xs, bank((7, 4)[hf]), ALU.add).then_inc(x_add, 1)
                        dve.reg_add(passes, passes, 1)

                    writes = dve.alloc_register("slot_cur_writes")
                    dve.reg_mov(writes, 1)
                    with dve.Fori(0, GROUPS) as g:
                        p_ = dve.value_load(npass[0:1, bass.ds(g, 1)], min_val=1, max_val=MAXPASS)
                        with dve.If(p_ > 1):
                            with dve.Fori(1, p_):
                                expert_pass(False, g)
                            V.tensor_copy(slot_cur[:], slot_no[:]).then_inc(slot_c, 1)
                            dve.reg_add(writes, writes, 1)
                        expert_pass(True, g)

            nc.gpsimd.sem_clear(range(first.num, last.num + 1))
            nc.all_engine_barrier()

        gain = br[:, 0, :, :].rearrange("p a n -> p (a n)")
        with nc.Block() as final:

            @final.sync
            def _(sp):
                sp.dma_start(gain, norm_f_g.rearrange("(o n) -> o n", o=1).broadcast_to([P, D]))\
                    .then_inc(once_loaded, 16)
                out_v = out[0].rearrange("(t p) d -> t p d", p=P)
                for t in range(TT):
                    sp.wait_ge(x_mid, t + 1)
                    sp.dma_start(out_v[t], wide[:, t, :]).then_inc(out_stored, 16)
                sp.wait_ge(out_stored, 16 * TT)

            @final.scalar
            def _(act):
                for t in range(TT):
                    nc.scalar.activation(wide[:, t, :], x[:, t, :], ACT.Square, accum_out=ss[:, t:t + 1])\
                        .then_inc(squares, 1)
                act.wait_ge(var_ready, 1)
                nc.scalar.activation(sd, var, ACT.Sqrt).then_inc(root, 1)

            @final.vector
            def _(dve):
                n = [0]

                def link(ins):
                    n[0] += 1
                    ins.then_inc(dve_c, 1)
                    dve.wait_ge(dve_c, n[0])

                V = nc.vector
                dve.wait_ge(squares, TT)
                link(V.tensor_scalar(var, ss, 1.0 / D, EPS, ALU.mult, ALU.add))
                V.tensor_scalar(nt, var, -0.5, None, ALU.mult).then_inc(var_ready, 1)
                dve.wait_ge(root, 1)
                dve.wait_ge(var_ready, 1)
                t2 = scal[:, 60:62]
                link(V.reciprocal(ir, sd))
                link(V.tensor_tensor(t2, ir, ir, ALU.mult))
                link(V.tensor_tensor(t2, t2, nt, ALU.mult))
                link(V.tensor_scalar(t2, t2, 1.5, None, ALU.add))
                link(V.tensor_tensor(ir, ir, t2, ALU.mult))
                dve.wait_ge(once_loaded, 16 * (NONCE + 1))
                for t in range(TT):
                    V.scalar_tensor_tensor(wide[:, t, :], x[:, t, :], ir[:, t:t + 1], gain, ALU.mult, ALU.mult)\
                        .then_inc(x_mid, 1)


_INS = ["x", "positions", "norm1_g", "w_in", "sgu_ln_g", "sgu_ln_b", "w_spatial", "b_spatial", "conv_w",
        "w_branch", "w_out", "norm2_g", "w_router_group", "b_router_group", "w_router_expert",
        "b_router_expert", "w_exp_gate", "w_exp_up", "w_exp_down", "norm_f_g"]


def kernel(**inputs):
    import numpy as _np
    import concourse.bacc as _bacc
    from concourse import mybir as _mybir
    from concourse.bass_utils import run_bass_kernel_spmd as _run

    nc = _bacc.Bacc("TRN2", target_bir_lowering=False, num_devices=1)
    arrays, args = {}, []
    for name in _INS:
        a = _np.ascontiguousarray(inputs[name])
        arrays[f"in_{name}"] = a
        args.append(nc.dram_tensor(f"in_{name}", a.shape, _mybir.dt.from_np(a.dtype), kind="ExternalInput").ap())
    args.append(nc.dram_tensor("out_0", (1, T, D), F32, kind="ExternalOutput").ap())
    build(nc, *args)
    r = _run(nc, [arrays], core_ids=[0])
    return r.results[0]["out_0"]
```

```python
import math
from contextlib import ExitStack

import numpy as np
import concourse.bass as bass
from concourse import mybir

F32 = mybir.dt.float32
F32R = mybir.dt.float32r
I32 = mybir.dt.int32
ACT = mybir.ActivationFunctionType
ALU = mybir.AluOpType
AX = mybir.AxisListType

D = 1024
T = 256
DEPTH = 2
P = 128
TT = T // P
C = D // P
BW = 256
HD = 64
NH = 4
IH, ID = 4, 32
TOPK = min(256, T // 4)
NE, NG, EG = 32, 4, 8
DE = 256
EPS = 1e-6
ROPE_THETA = 10000.0
ATT_SCALE = HD ** -0.5
MASKED = -1.0e30
TAKEN = -3.0e38

BLOCK_VI = (512, 420)
BLOCK_QK = (0, 512)
BLOCK_QKC = (1444, 512)
BLOCK_VB = (1956, 512)
BLOCK_CX = (2468, 512)
BLOCK_UV = (932, 512)
GATES = 2980
BRANCH_ORDER = (3, 1, 2, 0)

MIXER_UNITS = [("in", b[0], b[1], h)
               for b in (BLOCK_VI, BLOCK_QK, BLOCK_QKC, BLOCK_VB, BLOCK_CX, BLOCK_UV) for h in range(2)]
for _n in BRANCH_ORDER:
    MIXER_UNITS.append(("branch", _n))
    MIXER_UNITS += [("in", GATES + _n * D + 512 * _hf, 512, _h) for _hf in range(2) for _h in range(2)]
MIXER_UNITS += [("out", _u) for _u in range(4)]
NU = len(MIXER_UNITS)
LAST_UNIT = [1, 3, 5, 7, 9, 11]
for _j in range(4):
    LAST_UNIT += [12 + 5 * _j, 12 + 5 * _j, 14 + 5 * _j, 16 + 5 * _j]
RING = 12
MRING = 9
UNIT = 2048
HALF = UNIT // 2
SPLITS = 4
GE = 4
GROUPS = NE // GE
USE_ORDER = [(0, 0), (0, 1), (1, 0), (1, 1), (0, 2), (2, 0), (2, 1), (1, 2), (3, 0), (3, 1), (2, 2), (3, 2)]
SLOTS = 32
LOADS_LOW = NU // MRING + GROUPS
LOADS_HIGH = GROUPS
MAXPASS = T // SLOTS

PG1, PG2, PBS, PCW, PBR = 0, C, 2 * C, 2 * C + 4, 2 * C + 10
NSMALL = PBR + NG + NE


def build(nc, x_in, positions, norm1_g, w_in, sgu_ln_g, sgu_ln_b, w_spatial, b_spatial, conv_w, w_branch,
          w_out, norm2_g, w_rg, b_rg, w_re, b_re, w_eg, w_eu, w_ed, norm_f_g, out):
    ctx = ExitStack()
    with ctx:
        def sb(name, shape, dt=F32):
            return ctx.enter_context(nc.sbuf_tensor(name, shape, dt))

        ring = sb("ring", [P, RING * UNIT])
        split_hi = sb("split_hi", [P, SPLITS, HALF], F32R)
        split_lo = sb("split_lo", [P, SPLITS, HALF], F32R)
        x = sb("x", [P, TT, D])
        hT_hi = sb("hT_hi", [P, C, T], F32R)
        hT_lo = sb("hT_lo", [P, C, T], F32R)
        yT_hi = sb("yT_hi", [P, 2, 2, T], F32R)
        yT_lo = sb("yT_lo", [P, 2, 2, T], F32R)
        wide = sb("wide", [P, TT, D])
        qkr = sb("qkr", [P, TT, 512])
        tmpP = sb("tmpP", [P, TT, 512])
        idx = sb("idx", [P, TT, 256])
        br = sb("br", [P, 2, TT, 512])
        y_ab = sb("y_ab", [P, TT, BW])
        y_c = sb("y_c", [P, TT, BW])
        vc = sb("vc", [P, TT, BW])
        mb = sb("mb", [P, 384])
        small_all = sb("small_all", [P, DEPTH, NSMALL])
        small = sb("small", [P, NSMALL])
        lnp = sb("lnp", [P, 2, BW])
        ws = y_c[:, :, :].rearrange("p t n -> p (t n)").rearrange("p (g s) -> p g s", g=NG)
        wsT = sb("wsT", [P, NG, P])
        wr = sb("wr", [P, C, NG + NE])
        ident = sb("ident", [P, P])
        ones = sb("ones", [P, P])
        incl_T = sb("incl_T", [P, P])
        mask_a = sb("mask_a", [P, 2 * P])
        mask_c = sb("mask_c", [P, 2 * P])
        cos_a, sin_a = sb("cos_a", [P, TT, HD]), sb("sin_a", [P, TT, HD])
        cos_i, sin_i = sb("cos_i", [P, TT, ID]), sb("sin_i", [P, TT, ID])
        pos_i = sb("pos_i", [P, TT], I32)
        slot_no = sb("slot_no", [P, SLOTS])
        slot_cur = sb("slot_cur", [P, SLOTS])
        slots_on = sb("slots_on", [P, SLOTS])
        desc = sb("desc", [P, EG])
        limits = sb("limits", [P, MAXPASS])
        eps_t = sb("eps_t", [P, 1])
        scal = sb("scal", [P, 64])
        npass = sb("npass", [1, GROUPS], I32)
        bn = sb("bn", [P, TT, 6])
        wt = sb("wt", [P, TT, NE])
        rankm = sb("rankm", [P, TT, NE])

        def att(k):
            return ring[:, (MRING * 2 + k) * HALF:(MRING * 2 + k + 1) * HALF]
        qkT_a = att(0).rearrange("p (m t) -> p m t", m=4)
        zc = att(1).rearrange("p (h s) -> p h s", h=NH)
        sc = att(2).rearrange("p (h s) -> p h s", h=NH)
        pT = att(3).rearrange("p (b h q) -> p b h q", b=2, h=NH)
        uv = att(4).rearrange("p (t n) -> p t n", t=TT)
        vi = att(5)[:, 0:TT * 420].rearrange("p (t n) -> p t n", t=TT)
        iqT = br[:, 0, :, :].rearrange("p a n -> p (a n)").rearrange("p (h t) -> p h t", h=IH)
        qkT_c = br[:, 1, :, :].rearrange("p a n -> p (a n)").rearrange("p (m t) -> p m t", m=4)
        bdT = wide[:, 0, 0:512].rearrange("p (m t) -> p m t", m=2)
        ikT = wide[:, 0, 512:768]
        score_of = (mb[:, 0:P], mb[:, P:])
        cxT = tmpP[:, :, :].rearrange("p a n -> p (a n)").rearrange("p (m t) -> p m t", m=4)
        sig = qkr
        merged = wide
        vn = idx
        xn_hi = split_hi[:, 0:2, :]
        xn_lo = split_lo[:, 0:2, :]
        pick = split_hi[:, 3, 0:TT * P].rearrange("p (t s) -> p t s", t=TT)
        place_diff = idx[:, :, 0:P]
        wr_hi = split_hi[:, 2, 0:C * (NG + NE)].rearrange("p (c e) -> p c e", c=C)
        wr_lo = split_lo[:, 2, 0:C * (NG + NE)].rearrange("p (c e) -> p c e", c=C)
        hG = qkr[:, :, :].rearrange("p a n -> p (a n)").rearrange("p (c s) -> p c s", c=C)
        y_slots = tmpP[:, :, :].rearrange("p a n -> p (a n)")
        brf = br[:, :, :, :].rearrange("p a b n -> p (a b n)")
        wpick = brf[:, 0:256].rearrange("p (t s) -> p t s", t=TT)
        scatT = brf[:, 256:512].rearrange("p (t s) -> p t s", t=TT)
        hid = brf[0:SLOTS, 512:1024].rearrange("p (a f) -> p a f", a=2)
        silu = brf[:, 1024:1152].rearrange("p (a f) -> p a f", a=2)
        hidT = brf[:, 1152:1280].rearrange("p (a k s) -> p a k s", a=2, k=2)
        rl = brf[:, 1280:1280 + TT * 36].rearrange("p (t e) -> p t e", t=TT)
        member = brf[:, 1408:1472].rearrange("p (t e) -> p t e", t=TT)
        prod32 = brf[:, 1472:1536].rearrange("p (t g e) -> p t g e", t=TT, g=NG)
        rt = brf[:, 1536:1792]
        cnts = brf[:, 1792:1800]
        logitT = brf[0:NG + NE, 0:T]

        ps = ctx.enter_context(nc.psum_tensor("ps", [P, 8, 512], F32))

        def sem(name):
            return ctx.enter_context(nc.semaphore(name))

        ring_loaded = [sem(f"ring_loaded{i}") for i in range(RING)]
        x_loaded, pos_loaded, once_loaded = sem("x_loaded"), sem("pos_loaded"), sem("once_loaded")
        layer_loaded = sem("layer_loaded")
        out_stored = sem("out_stored")
        tab = sem("tab")
        first = sem("layer_first")
        hi_done, lo_done, half_used = sem("hi_done"), sem("lo_done"), sem("half_used")
        small_ready = sem("small_ready")
        squares, root, inv_rms = sem("squares"), sem("root"), sem("inv_rms")
        xn_dve, xn_act = sem("xn_dve"), sem("xn_act")
        xT_mm, xT_hi, xT_lo = sem("xT_mm"), sem("xT_hi"), sem("xT_lo")
        ws_T, ws_ready = sem("ws_T"), sem("ws_ready")
        block_out = sem("block_out")
        rot_i, rot_a, pool_c = sem("rot_i"), sem("rot_a"), sem("pool_c")
        idx_T, idx_out, rel_mm, rel_out = sem("idx_T"), sem("idx_out"), sem("rel_mm"), sem("rel_out")
        qk_T, qk_out, mb_done = sem("qk_T"), sem("qk_out"), sem("mb_done")
        zc_mm, zc_out, zabs, zln, zarg, zexp = (sem("zc_mm"), sem("zc_out"), sem("zabs"), sem("zln"),
                                               sem("zarg"), sem("zexp"))
        pT_mm, pT_out, pv_mm, y_out = sem("pT_mm"), sem("pT_out"), sem("pv_mm"), sem("y_out")
        conv_y, gelu_out = sem("conv_y"), sem("gelu_out")
        ln_var, ln_root, vn_dve, vn_done = sem("ln_var"), sem("ln_root"), sem("vn_dve"), sem("vn_done")
        sgu_mm, yb_done = sem("sgu_mm"), sem("yb_done")
        yT_mm, yT_hi_out, yT_lo_out = sem("yT_mm"), sem("yT_hi_out"), sem("yT_lo_out")
        la_mm, la_out, la_max, la_exp, la_sum = (sem("la_mm"), sem("la_out"), sem("la_max"), sem("la_exp"),
                                                sem("la_sum"))
        gate_prod, gate_sum = sem("gate_prod"), sem("gate_sum")
        mid_mm, x_mid = sem("mid_mm"), sem("x_mid")
        wr_hi_out, wr_lo_out, route_mm = sem("wr_hi_out"), sem("wr_lo_out"), sem("route_mm")
        logitT_out, logit_T = sem("logitT_out"), sem("logit_T")
        xs_hi, xs_lo = sem("xs_hi"), sem("xs_lo")
        gmax, gexp, emax, eexp = sem("gmax"), sem("gexp"), sem("emax"), sem("eexp")
        member_ok, rank_mm, passes_ok, routed = (sem("member_ok"), sem("rank_mm"), sem("passes_ok"),
                                                 sem("routed"))
        dve_c = sem("dve_c")
        diff_ok, pick_ok, wpick_ok, slot_c = sem("diff_ok"), sem("pick_ok"), sem("wpick_ok"), sem("slot_c")
        gath_mm, gath_out = sem("gath_mm"), sem("gath_out")
        scat_T = sem("scat_T")
        gu_mm, silu_out, hid_out, hid_T, hidT_out = (sem("gu_mm"), sem("silu_out"), sem("hid_out"),
                                                     sem("hid_T"), sem("hidT_out"))
        down_mm, y_act, y_dve = sem("down_mm"), sem("y_act"), sem("y_dve")
        scat_mm, x_add = sem("scat_mm"), sem("x_add")
        unit_used = sem("unit_used")
        last = sem("layer_last")

        w_in_v = w_in.rearrange("l (p c) n -> l p c n", c=C)
        w_br_v = w_branch.rearrange("l b (k p) n -> l b p k n", p=P)
        w_out_v = w_out.rearrange("l (c p) n -> l p c n", p=P)
        w_eg_v = w_eg.rearrange("l e (p c) f -> (l e) p c f", c=C)
        w_eu_v = w_eu.rearrange("l e (p c) f -> (l e) p c f", c=C)
        w_ed_v = w_ed.rearrange("l e (p k) d -> (l e) p k d", k=2)

        def slot(s):
            return ring[:, s * UNIT:(s + 1) * UNIT]

        def unit_cols(u):
            return MIXER_UNITS[u][2] if MIXER_UNITS[u][0] == "in" else D

        def half_view(buf, v):
            n = unit_cols(v // 2)
            if n == D:
                return buf.rearrange("p (k n) -> p k n", k=1)
            return buf.rearrange("p (k n) -> p k n", k=2)[:, :, 0:n]

        def raw_half(v):
            s = (v // 2) % MRING
            return half_view(ring[:, s * UNIT + (v % 2) * HALF:s * UNIT + (v % 2 + 1) * HALF], v)

        def load_mixer_unit(sp, u, l):
            kind = MIXER_UNITS[u]
            s = u % MRING
            if kind[0] == "in":
                _, c0, n, h = kind
                dst = slot(s).rearrange("p (k n) -> p k n", k=4)[:, :, 0:n]
                src = w_in_v[l][:, 4 * h:4 * h + 4, c0:c0 + n]
            elif kind[0] == "branch":
                dst = slot(s).rearrange("p (k n) -> p k n", k=2)
                src = w_br_v[l][kind[1]]
            else:
                dst = slot(s).rearrange("p (k n) -> p k n", k=2)
                src = w_out_v[l][:, 2 * kind[1]:2 * kind[1] + 2, :]
            sp.dma_start(dst, src).then_inc(ring_loaded[s], 16)

        def load_expert_unit(sp, le, i, part):
            s = 3 * i + part
            if part < 2:
                dst = slot(s).rearrange("p (c f) -> p c f", c=C)
                src = (w_eg_v if part == 0 else w_eu_v)[le]
            else:
                dst = slot(s).rearrange("p (k d) -> p k d", k=2)
                src = w_ed_v[le]
            sp.dma_start(dst, src).then_inc(ring_loaded[s], 16)

        inv_freq = (ROPE_THETA ** (-np.arange(0, HD, 2) / HD)).astype(np.float32)
        SMALL_LOADS = 4 + 3 * DEPTH
        ang, red, freq = brf[:, 0:64], brf[:, 64:128], brf[:, 128:160]
        posf = scal[:, 0:TT]

        ss, var, sd, ir, nt = (scal[:, 2 * i:2 * i + 2] for i in range(1, 6))
        top8 = scal[:, 16:24]
        lmax, lneg, lsum, linv = (scal[:, 24 + 4 * i:28 + 4 * i] for i in range(4))
        lmv = scal[:, 40:44].rearrange("p (t k) -> p t k", t=TT)
        lvar, lsd, lrs = scal[:, 44:46], scal[:, 46:48], scal[:, 48:50]
        spare, t2 = scal[:, 58:59], scal[:, 60:62]

        def square_of_x(t):
            nc.scalar.activation(wide[:, t, :], x[:, t, :], ACT.Square, accum_out=ss[:, t:t + 1]).then_inc(squares, 1)

        def preload_sqrt():
            nc.scalar.activation(spare, eps_t[:], ACT.Sqrt)

        def root_of_mean(act, k):
            act.wait_ge(squares, 2 * k)
            nc.scalar.activation(sd, ss, ACT.Sqrt, bias=eps_t[:], scale=1.0 / D).then_inc(root, 1)

        def newton(link, r, s_, mhalf_v):
            link(nc.vector.reciprocal(r, s_))
            link(nc.vector.tensor_tensor(t2, r, r, ALU.mult))
            link(nc.vector.tensor_tensor(t2, t2, mhalf_v, ALU.mult))
            return nc.vector.scalar_tensor_tensor(r, t2, 1.5, r, ALU.add, ALU.mult)

        def inverse_rms(dve, link, k):
            dve.wait_ge(squares, 2 * k)
            link(nc.vector.tensor_scalar(var, ss, 1.0 / D, EPS, ALU.mult, ALU.add))
            link(nc.vector.tensor_scalar(nt, var, -0.5, None, ALU.mult))
            dve.wait_ge(root, k)
            newton(link, ir, sd, nt).then_inc(inv_rms, 1)

        def keep_warm(k, bank_no):
            for _ in range(k):
                nc.tensor.matmul(ps[:, bank_no, 0:P], ones[:], ident[:], start=True, stop=True,
                                 skip_group_check=True)

        with nc.Block() as once:

            @once.tensor
            def _(pe):
                pe.wait_ge(pool_c, 2)
                keep_warm(24, 3)

            @once.sync
            def _(sp):
                x_v = x_in[0].rearrange("(t p) d -> t p d", p=P)
                for t in range(TT):
                    sp.dma_start(x[:, t, :], x_v[t]).then_inc(x_loaded, 16)
                sp.dma_start(pos_i[:], positions[0].rearrange("(t p) -> p t", p=P),
                             allow_slow_non_contiguous=True).then_inc(pos_loaded, 16)

                def small_load(at, src, layers=slice(0, DEPTH)):
                    w = src.shape[2]
                    sp.dma_start(small_all[:, layers, at:at + w], src, allow_slow_non_contiguous=True)\
                        .then_inc(once_loaded, 16)

                small_load(PG1, norm1_g.rearrange("l (p c) -> p l c", c=C))
                load_mixer_unit(sp, 0, 0)
                load_mixer_unit(sp, 1, 0)
                small_load(PG2, norm2_g.rearrange("l (p c) -> p l c", c=C))
                for layer_no in range(DEPTH):
                    one = slice(layer_no, layer_no + 1)
                    small_load(PBS, b_spatial[one].rearrange("l g t -> t l g"), one)
                    for k in range(2):
                        small_load(PCW + 3 * k, conv_w[one, :, P * k:P * k + P].rearrange("l w p -> p l w"), one)
                small_load(PBR, b_rg.rearrange("(o l) e -> o l e", o=1).broadcast_to([P, DEPTH, NG]))
                small_load(PBR + NG, b_re.rearrange("(o l) e -> o l e", o=1).broadcast_to([P, DEPTH, NE]))
                for u in range(2, MRING):
                    load_mixer_unit(sp, u, 0)

            @once.scalar
            def _(act):
                act.wait_ge(tab, 1)
                nc.scalar.activation(ang, ang, ACT.Sin).then_inc(tab, 1)
                nc.scalar.activation(red, red, ACT.Sin).then_inc(tab, 1)
                act.wait_ge(x_loaded, 16 * TT)
                act.wait_ge(pool_c, 1)
                preload_sqrt()
                for t in range(TT):
                    square_of_x(t)
                root_of_mean(act, 1)

            @once.gpsimd
            def _(pool):
                for i in range(HD // 2):
                    nc.gpsimd.memset(freq[:, i:i + 1], float(inv_freq[i]))
                for i in range(EG):
                    nc.gpsimd.memset(desc[:, i:i + 1], float(EG - i))
                nc.gpsimd.memset(eps_t[:], EPS)
                nc.gpsimd.memset(slots_on[:], float(SLOTS))
                for i in range(MAXPASS):
                    nc.gpsimd.memset(limits[:, i:i + 1], float(SLOTS * i) if i else -1.0)
                nc.gpsimd.memset(mask_a[:], 0.0)
                nc.gpsimd.memset(mask_c[:], 0.0)
                nc.gpsimd.memset(ones[:], 1.0).then_inc(pool_c, 1)
                pool.wait_ge(pool_c, 1)
                nc.gpsimd.iota(slot_no[:], pattern=[[1, SLOTS]], base=1, channel_multiplier=0,
                               allow_small_or_imprecise_dtypes=True)
                nc.gpsimd.affine_select(out=ident[:], in_=ones[:], compare_op=ALU.is_equal, fill=0.0, base=0,
                                        pattern=[[-1, P]], channel_multiplier=1)
                nc.gpsimd.affine_select(out=incl_T[:], in_=ones[:], compare_op=ALU.is_ge, fill=0.0, base=0,
                                        pattern=[[1, P]], channel_multiplier=-1)
                nc.gpsimd.affine_select(out=mask_a[:, P:], in_=mask_a[:, P:], compare_op=ALU.is_ge, fill=MASKED,
                                        base=0, pattern=[[-1, P]], channel_multiplier=1)
                nc.gpsimd.affine_select(out=mask_c[:, P:], in_=mask_c[:, P:], compare_op=ALU.is_gt, fill=MASKED,
                                        base=0, pattern=[[-1, P]], channel_multiplier=1).then_inc(pool_c, 1)

            @once.vector
            def _(dve):
                n = [0]

                def link(ins):
                    n[0] += 1
                    ins.then_inc(dve_c, 1)
                    dve.wait_ge(dve_c, n[0])

                dve.wait_ge(pos_loaded, 16)
                dve.wait_ge(pool_c, 1)
                link(nc.vector.tensor_copy(posf, pos_i[:]))
                for t in range(TT):
                    link(nc.vector.tensor_scalar(ang[:, 32 * t:32 * t + 32], freq, posf[:, t:t + 1], None,
                                                 ALU.mult))
                magic = 12582912.0
                c1, c2 = 6.28125, 0.0019350051879882812
                c3 = 2 * math.pi - c1 - c2
                link(nc.vector.tensor_scalar(red, ang, 1 / (2 * math.pi), magic, ALU.mult, ALU.add))
                link(nc.vector.tensor_scalar(red, red, magic, None, ALU.subtract))
                for c in (c1, c2, c3):
                    link(nc.vector.scalar_tensor_tensor(ang, red, -c, ang, ALU.mult, ALU.add))
                link(nc.vector.tensor_scalar(ang, ang, 3.141592, -3.141592, ALU.min, ALU.max))
                link(nc.vector.tensor_scalar(red, ang, math.pi / 2, None, ALU.add))
                tmp = brf[:, 160:224]
                link(nc.vector.tensor_scalar(tmp, red, math.pi, 2 * math.pi, ALU.is_gt, ALU.mult))
                link(nc.vector.tensor_tensor(red, red, tmp, ALU.subtract))
                link(nc.vector.tensor_scalar(red, red, 3.141592, -3.141592, ALU.min, ALU.max))
                nc.vector.tensor_scalar(posf, posf, 1.0, None, ALU.mult).then_inc(tab, 1)
                dve.wait_ge(tab, 3)
                s3 = ang.rearrange("p (t f) -> p t f", t=TT)
                c3_ = red.rearrange("p (t f) -> p t f", t=TT)
                for h in range(2):
                    nc.vector.tensor_copy(cos_a[:, :, 32 * h:32 * h + 32], c3_)
                    nc.vector.tensor_scalar(sin_a[:, :, 32 * h:32 * h + 32], s3, 2.0 * h - 1.0, None, ALU.mult)
                    nc.vector.tensor_copy(cos_i[:, :, 16 * h:16 * h + 16], c3_[:, :, ::2])
                    nc.vector.tensor_scalar(sin_i[:, :, 16 * h:16 * h + 16], s3[:, :, ::2], 2.0 * h - 1.0, None,
                                            ALU.mult)
                inverse_rms(dve, link, 1)
        nc.gpsimd.sem_clear(range(first.num, last.num + 1))
        nc.all_engine_barrier()

        xp = [x[:, t, :].rearrange("p (q c) -> p c q", c=C) for t in range(TT)]
        xnp = [wide[:, t, :].rearrange("p (c q) -> p c q", c=C) for t in range(TT)]

        def bank(b, n=1):
            return ps[:, b, :] if n == 1 else ps[:, b:b + n, :]

        with nc.Fori(0, DEPTH) as l:
            with nc.Block() as layer:

                @layer.sync
                def _(sp):
                    for u in range(MRING, NU):
                        sp.wait_ge(lo_done, 2 * (u - MRING + 1))
                        load_mixer_unit(sp, u, l)
                    for i in range(GE):
                        for part in range(3):
                            s = 3 * i + part
                            if s < MRING:
                                sp.wait_ge(lo_done, 2 * (NU - MRING + s + 1))
                            elif s == MRING:
                                sp.wait_ge(pv_mm, 4)
                            load_expert_unit(sp, l * NE + i, i, part)
                    with sp.Fori(1, GROUPS) as g:
                        for k, (i, part) in enumerate(USE_ORDER):
                            sp.wait_ge(unit_used, g * RING + (k + 1 - RING))
                            load_expert_unit(sp, l * NE + g * GE + i, i, part)
                    with sp.If(l < DEPTH - 1):
                        after = nc.s_assert_within(l + 1, 0, DEPTH - 1, skip_runtime_bounds_check_because=
                                                   "only where a layer follows")
                        for u in range(MRING):
                            sp.wait_ge(unit_used, (GROUPS - 1) * RING + USE_ORDER.index((u // 3, u % 3)) + 1)
                            load_mixer_unit(sp, u, after)

                @layer.gpsimd
                def _(pool):
                    n = [0]

                    def link(ins):
                        n[0] += 1
                        ins.then_inc(pool_c, 1)
                        return n[0]

                    for k, src in enumerate((sgu_ln_g, sgu_ln_b)):
                        pool.dma_start(lnp[:, k, :], src[l].rearrange("(o n) -> o n", o=1)
                                       .broadcast_to([P, BW])).then_inc(layer_loaded, 16)
                    pool.dma_start(ws, w_spatial[l].rearrange("g t s -> t g s")).then_inc(layer_loaded, 16)
                    pool.dma_start(wr[:, :, 0:NG], w_rg[l].rearrange("(p c) e -> p c e", c=C))\
                        .then_inc(layer_loaded, 16)
                    pool.dma_start(wr[:, :, NG:], w_re[l].rearrange("(p c) e -> p c e", c=C))\
                        .then_inc(layer_loaded, 16)
                    nc.gpsimd.memset(iqT, 0.0).then_inc(first, 1)

                    pool.wait_ge(block_out, 1)
                    H5 = IH + 1
                    for t in range(TT):
                        src = vi[:, t, 256:416].rearrange("p (h s f) -> p h s f", h=H5, s=2)
                        full = vi[:, t, 256:416].rearrange("p (h f) -> p h f", h=H5)
                        a = tmpP[:, t, 0:160].rearrange("p (h f) -> p h f", h=H5)
                        b = tmpP[:, t, 160:320].rearrange("p (h s f) -> p h s f", h=H5, s=2)
                        bf = tmpP[:, t, 160:320].rearrange("p (h f) -> p h f", h=H5)
                        nc.gpsimd.tensor_tensor(a, full, cos_i[:, t:t + 1, :].broadcast_to([P, H5, ID]), ALU.mult)
                        nc.gpsimd.tensor_tensor(b[:, :, 0, :], src[:, :, 1, :],
                                                sin_i[:, t:t + 1, 0:16].broadcast_to([P, H5, 16]), ALU.mult)
                        k = link(nc.gpsimd.tensor_tensor(b[:, :, 1, :], src[:, :, 0, :],
                                                         sin_i[:, t:t + 1, 16:32].broadcast_to([P, H5, 16]),
                                                         ALU.mult))
                        pool.wait_ge(pool_c, k)
                        nc.gpsimd.tensor_tensor(idx[:, t, 0:128].rearrange("p (h f) -> p h f", h=IH),
                                                a[:, 0:IH, :], bf[:, 0:IH, :], ALU.add)
                        nc.gpsimd.tensor_tensor(idx[:, t, 128:256].rearrange("p (h f) -> p h f", h=IH),
                                                a[:, IH:H5, :].broadcast_to([P, IH, ID]),
                                                bf[:, IH:H5, :].broadcast_to([P, IH, ID]), ALU.add)\
                            .then_inc(rot_i, 1)
                    pool.wait_ge(block_out, 2)
                    pool.wait_ge(rot_i, 2)
                    H8 = 2 * NH
                    for t in range(TT):
                        src = uv[:, t, :].rearrange("p (h s f) -> p h s f", h=H8, s=2)
                        full = uv[:, t, :].rearrange("p (h f) -> p h f", h=H8)
                        a = tmpP[:, t, :].rearrange("p (h f) -> p h f", h=H8)
                        b = qkr[:, t, :].rearrange("p (h s f) -> p h s f", h=H8, s=2)
                        nc.gpsimd.tensor_tensor(a, full, cos_a[:, t:t + 1, :].broadcast_to([P, H8, HD]), ALU.mult)
                        nc.gpsimd.tensor_tensor(b[:, :, 0, :], src[:, :, 1, :],
                                                sin_a[:, t:t + 1, 0:32].broadcast_to([P, H8, 32]), ALU.mult)
                        k = link(nc.gpsimd.tensor_tensor(b[:, :, 1, :], src[:, :, 0, :],
                                                         sin_a[:, t:t + 1, 32:64].broadcast_to([P, H8, 32]),
                                                         ALU.mult))
                        pool.wait_ge(pool_c, k)
                        nc.gpsimd.tensor_tensor(qkr[:, t, :], tmpP[:, t, :], qkr[:, t, :], ALU.add)\
                            .then_inc(rot_a, 1)
                    pool.wait_ge(layer_loaded, 16 * 5 * (l + 1))
                    pool.wait_ge(vn_dve, 1)
                    k = link(nc.gpsimd.tensor_tensor(vn[:], vn[:], lnp[:, 0:1, :].broadcast_to([P, TT, BW]),
                                                     ALU.mult))
                    pool.wait_ge(pool_c, k)
                    nc.gpsimd.tensor_tensor(vn[:], vn[:], lnp[:, 1:2, :].broadcast_to([P, TT, BW]), ALU.add)\
                        .then_inc(vn_done, 1)
                    for j in range(2, 7):
                        hf = j % 2
                        pool.wait_ge(gate_prod, j + 1)
                        m = merged[:, :, 512 * hf:512 * hf + 512]
                        nc.gpsimd.tensor_tensor(m, m, sig[:], ALU.add).then_inc(gate_sum, 1)
                    pool.wait_ge(x_mid, 1)
                    nc.gpsimd.memset(scatT, 0.0).then_inc(y_act, 1)
                    nc.gpsimd.memset(y_slots, 0.0).then_inc(y_dve, 1)
                    nc.gpsimd.tensor_tensor(slot_cur[:], slot_no[:], ones[:, 0:SLOTS], ALU.mult).then_inc(slot_c, 1)
                    pool.wait_ge(xs_hi, 1)
                    nc.gpsimd.tensor_tensor(xn_lo[:, 1, :], wide[:, 1, :], xn_hi[:, 1, :].bitcast(F32), ALU.subtract)\
                        .then_inc(xs_lo, 1)
                    pool.wait_ge(passes_ok, 1)
                    pool.sem_inc(pick_ok, 1)

                    passes = pool.alloc_register("pool_passes")
                    pool.reg_mov(passes, 0)
                    writes = pool.alloc_register("slot_cur_writes")
                    pool.reg_mov(writes, 1)

                    def diff(places, n, g):
                        pool.wait_ge(pick_ok, n + 1)
                        for t in range(TT):
                            ins = nc.gpsimd.tensor_tensor(place_diff[:, t, :].rearrange("p (i s) -> p i s", i=GE),
                                                          rankm[:, t, bass.ds(g * GE, GE)]
                                                          .rearrange("p (i o) -> p i o", o=1)
                                                          .broadcast_to([P, GE, SLOTS]),
                                                          places[:].rearrange("p (o s) -> p o s", o=1)
                                                          .broadcast_to([P, GE, SLOTS]), ALU.subtract)
                        ins.then_inc(diff_ok, 1)

                    def expert_pass(main, g):
                        n = pool.snap(passes)
                        places = slot_no
                        if not main:
                            pool.wait_ge(slot_c, pool.snap(writes))
                            nc.gpsimd.tensor_tensor(slot_cur[:], slot_cur[:], slots_on[:], ALU.add)\
                                .then_inc(slot_c, 1)
                            pool.reg_add(writes, writes, 1)
                            pool.wait_ge(slot_c, pool.snap(writes))
                            places = slot_cur
                        diff(places, n, g)
                        pool.wait_ge(scat_T, n + 1)
                        pool.wait_ge(pick_ok, n + 2)
                        for t in range(TT):
                            ins = nc.gpsimd.tensor_tensor(wpick[:, t, :].rearrange("p (i s) -> p i s", i=GE),
                                                          pick[:, t, :].rearrange("p (i s) -> p i s", i=GE)
                                                          .bitcast(F32),
                                                          wt[:, t, bass.ds(g * GE, GE)]
                                                          .rearrange("p (i o) -> p i o", o=1)
                                                          .broadcast_to([P, GE, SLOTS]), ALU.mult)
                        ins.then_inc(wpick_ok, 1)
                        pool.reg_add(passes, passes, 1)

                    with pool.Fori(0, GROUPS) as g:
                        p_ = pool.value_load(npass[0:1, bass.ds(g, 1)], min_val=1, max_val=MAXPASS)
                        with pool.If(p_ > 1):
                            with pool.Fori(1, p_):
                                expert_pass(False, g)
                            nc.gpsimd.tensor_tensor(slot_cur[:], slot_no[:], ones[:, 0:SLOTS], ALU.mult)\
                                .then_inc(slot_c, 1)
                            pool.reg_add(writes, writes, 1)
                        expert_pass(True, g)
                    diff(slot_no, pool.snap(passes), 0)

                @layer.tensor
                def _(pe):
                    mm = nc.tensor.matmul

                    def transposes(dsts, srcs, done, idn=None):
                        for k, (d_, s_) in enumerate(zip(dsts, srcs)):
                            ins = nc.tensor.transpose(d_, s_, ident[:] if idn is None else idn)
                        ins.then_inc(done, 1)

                    def three(dst, st, mv, start, stop):
                        mm(dst, st[0], mv[0], start=start, stop=False, skip_group_check=True)
                        mm(dst, st[0], mv[1], start=False, stop=False, skip_group_check=True)
                        return mm(dst, st[1], mv[0], start=False, stop=stop, skip_group_check=True)

                    def h_tile(c, t=None):
                        cols = slice(0, T) if t is None else slice(P * t, P * t + P)
                        return hT_hi[:, c, cols], hT_lo[:, c, cols]

                    def w_tile(v, k, c0, n):
                        return (half_view(split_hi[:, v % SPLITS, :], v)[:, k, c0:c0 + n],
                                half_view(split_lo[:, v % SPLITS, :], v)[:, k, c0:c0 + n])

                    def in_half(v, use, layout):
                        b0 = 2 * (use % 2)
                        h = MIXER_UNITS[v // 2][3]
                        n = unit_cols(v // 2)
                        pe.wait_ge(lo_done, v + 1)
                        if v < 4:
                            pe.wait_ge(xT_lo, v + 1)
                        chunks = [(4 * h + 2 * (v % 2) + k, k) for k in range(2)]
                        begin, end = chunks[0][0] == 0, chunks[-1][0] == C - 1
                        if begin and use >= 2:
                            pe.wait_ge(block_out, use - 1)
                        outs = []
                        if layout == "natural":
                            for t in range(TT):
                                outs.append((ps[:, b0 + t, 0:n], lambda c, k, t=t: h_tile(c, t),
                                             lambda c, k: w_tile(v, k, 0, n), True))
                        elif layout == "transposed":
                            for m in range(4):
                                outs.append((ps[:, b0 + m // 2, T * (m % 2):T * (m % 2) + T],
                                             lambda c, k, m=m: w_tile(v, k, P * m, P),
                                             lambda c, k: h_tile(c), m % 2 == 0))
                        else:
                            for t in range(TT):
                                outs.append((ps[:, b0, BW * t:BW * t + BW], lambda c, k, t=t: h_tile(c, t),
                                             lambda c, k: w_tile(v, k, 0, BW), t == 0))
                            for m in range(2):
                                outs.append((ps[:, b0 + 1, T * m:T * m + T],
                                             lambda c, k, m=m: w_tile(v, k, BW + P * m, P),
                                             lambda c, k: h_tile(c), m == 0))
                        for dst, st, mv, opens in outs:
                            for c, k in chunks:
                                ins = three(dst, st(c, k), mv(c, k), begin and k == 0 and opens,
                                            end and k == 1)
                        ins.then_inc(half_used, 1)

                    def in_unit(u, use, layout="natural"):
                        in_half(2 * u, use, layout)
                        in_half(2 * u + 1, use, layout)

                    def wide_unit(u, use, st, first_, last_):
                        for v in (2 * u, 2 * u + 1):
                            pe.wait_ge(lo_done, v + 1)
                            final_half = v == 2 * NU - 1
                            order = [(hf, t) for hf in range(2) for t in range(TT)]
                            if final_half:
                                order.sort(key=lambda o: o[1])
                            for n, (hf, t) in enumerate(order):
                                if first_ and v % 2 == 0 and t == 0:
                                    pe.wait_ge(block_out, use + hf - 1)
                                ins = three(ps[:, 2 * hf + t, :], st(v % 2, t), w_tile(v, 0, 512 * hf, 512),
                                            first_ and v % 2 == 0, last_ and v % 2 == 1)
                                if final_half and n == 1:
                                    ins.then_inc(mid_mm, 1)
                            ins.then_inc(half_used, 1)

                    def x_transposes(done0):
                        for b in range(4):
                            transposes([ps[:, 4 + b, T * k + P * t:T * k + P * t + P]
                                        for k in range(2) for t in range(TT)],
                                       [wide[:, t, P * (2 * b + k):P * (2 * b + k) + P]
                                        for k in range(2) for t in range(TT)], xT_mm)

                    def logits(qk, t, b0, done):
                        w = P * (t + 1)
                        for m in range(2):
                            for r in range(2):
                                ins = mm(ps[:, b0 + r, 256 * m:256 * m + w],
                                         qk[HD * r:HD * r + HD, m, P * t:P * t + P],
                                         qk[HD * r:HD * r + HD, 2 + m, 0:w], start=(m == 0), stop=True,
                                         skip_group_check=True)
                        ins.then_inc(done, 1)

                    def p_transposes(src, t, b0):
                        for b in range(t + 1):
                            for h in range(NH):
                                ins = nc.tensor.transpose(ps[:, b0 + b, P * h:P * h + P],
                                                          src[:, h, P * b:P * b + P], ident[:])
                        ins.then_inc(pT_mm, 1)

                    def pv(v, t, b0):
                        for s_, h in enumerate((0, 2, 1, 3)):
                            for b in range(t + 1):
                                ins = mm(ps[:, b0, HD * h:HD * h + HD], pT[:, b, s_, :],
                                         v[:, b, HD * h:HD * h + HD], start=(b == 0), stop=(b == t),
                                         skip_group_check=True)
                        ins.then_inc(pv_mm, 1)

                    def y_transposes(y, b0):
                        transposes([ps[:, b0, T * k + P * t:T * k + P * t + P]
                                    for k in range(2) for t in range(TT)],
                                   [y[:, t, P * k:P * k + P] for k in range(2) for t in range(TT)], yT_mm)

                    def y_tile(ring_at):
                        return lambda k, t: (yT_hi[:, ring_at, k, P * t:P * t + P],
                                             yT_lo[:, ring_at, k, P * t:P * t + P])

                    keep_warm(6, 3)
                    pe.wait_ge(xn_dve, 1)
                    pe.wait_ge(xn_act, 1)
                    x_transposes(0)
                    in_unit(0, 0)
                    in_unit(1, 0)
                    in_unit(2, 1)
                    in_unit(3, 1)
                    pe.wait_ge(layer_loaded, 16 * 5 * (l + 1))
                    transposes([ps[:, 4, P * g:P * g + P] for g in range(NG)], [ws[:, g, :] for g in range(NG)],
                               ws_T)
                    pe.wait_ge(rot_i, 2)
                    transposes([ps[:, 5, T * k + P * t:T * k + P * t + P] for k in range(2) for t in range(TT)],
                               [idx[:, t, P * k:P * k + P] for k in range(2) for t in range(TT)], idx_T)
                    in_unit(4, 2, "transposed")
                    in_unit(5, 2, "transposed")
                    pe.wait_ge(idx_out, 1)
                    pe.wait_ge(ws_ready, 1)
                    for t, b0 in ((0, 4), (1, 6)):
                        w = P * (t + 1)
                        for h in range(IH):
                            dst = ps[:, 4, P * h:P * h + P] if t == 0 else ps[:, 6 + h // 2,
                                                                             T * (h % 2):T * (h % 2) + T]
                            ins = mm(dst, iqT[:, h, P * t:P * t + P], ikT[:, 0:w], start=True, stop=True,
                                     skip_group_check=True)
                        ins.then_inc(rel_mm, 1)
                    pe.wait_ge(rot_a, 2)
                    pe.wait_ge(rel_out, 1)
                    for m in range(4):
                        for t in range(TT):
                            ins = nc.tensor.transpose(ps[:, 4 + m // 2, T * (m % 2) + P * t:T * (m % 2) + P * t + P],
                                                      qkr[:, t, P * m:P * m + P], ident[:])
                    ins.then_inc(qk_T, 1)
                    in_unit(6, 3, "mixed")
                    in_unit(7, 3, "mixed")
                    pe.wait_ge(rel_out, 2)
                    pe.wait_ge(block_out, 3)
                    logits(qkT_c, 0, 6, zc_mm)
                    in_unit(8, 4, "transposed")
                    in_unit(9, 4, "transposed")
                    pe.wait_ge(qk_out, 1)
                    logits(qkT_c, 1, 4, zc_mm)
                    in_unit(10, 5)
                    in_unit(11, 5)

                    pe.wait_ge(yT_lo_out, 1)
                    wide_unit(12, 6, y_tile(0), True, True)
                    in_unit(13, 8)
                    pe.wait_ge(zexp, 1)
                    pe.wait_ge(zc_out, 1)
                    p_transposes(zc, 0, 6)
                    in_unit(14, 8)
                    pe.wait_ge(pT_out, 1)
                    pv(vc, 0, 7)
                    pe.wait_ge(vn_done, 1)
                    for g in range(NG):
                        ins = mm(ps[:, 6, P * g:P * g + P], wsT[:, g, :], vn[:, :, HD * g:HD * g + HD],
                                 start=(g == 0), stop=True, skip_group_check=True)
                    ins.then_inc(sgu_mm, 1)
                    in_unit(15, 9)
                    pe.wait_ge(zexp, 2)
                    p_transposes(zc, 1, 4)
                    pe.wait_ge(yb_done, 1)
                    y_transposes(y_ab, 6)
                    in_unit(16, 9)
                    pe.wait_ge(pT_out, 2)
                    pe.wait_ge(y_out, 1)
                    pv(vc, 1, 7)
                    pe.wait_ge(yT_lo_out, 2)
                    wide_unit(17, 10, y_tile(1), True, True)
                    pe.wait_ge(y_out, 2)
                    y_transposes(y_c, 5)
                    logits(qkT_a, 0, 6, la_mm)
                    in_unit(18, 12)
                    pe.wait_ge(yT_lo_out, 3)
                    logits(qkT_a, 1, 4, la_mm)
                    in_unit(19, 12)
                    in_unit(20, 13)
                    pe.wait_ge(la_exp, 1)
                    p_transposes(sc, 0, 6)
                    in_unit(21, 13)
                    pe.wait_ge(pT_out, 3)
                    pv(vi, 0, 7)
                    pe.wait_ge(la_exp, 2)
                    p_transposes(zc, 1, 4)
                    wide_unit(22, 14, y_tile(0), True, True)
                    in_unit(23, 16)
                    pe.wait_ge(pT_out, 4)
                    pe.wait_ge(y_out, 3)
                    pv(vi, 1, 7)
                    in_unit(24, 16)
                    pe.wait_ge(y_out, 4)
                    y_transposes(y_ab, 6)
                    in_unit(25, 17)
                    in_unit(26, 17)
                    pe.wait_ge(yT_lo_out, 4)
                    wide_unit(27, 18, y_tile(1), True, True)
                    in_unit(28, 20)
                    in_unit(29, 20)
                    in_unit(30, 21)
                    pe.wait_ge(gate_sum, 5)

                    def m_transposes(c0):
                        for b in range(2):
                            transposes([ps[:, 4 + c0 // 2 + b, T * k + P * t:T * k + P * t + P]
                                        for k in range(2) for t in range(TT)],
                                       [merged[:, t, P * (c0 + 2 * b + k):P * (c0 + 2 * b + k) + P]
                                        for k in range(2) for t in range(TT)], xT_mm)

                    m_transposes(0)
                    in_unit(31, 21)
                    pe.wait_ge(xT_lo, 6)

                    def m_tile(u):
                        if u < 2:
                            return lambda k, t: (yT_hi[:, u, k, P * t:P * t + P], yT_lo[:, u, k, P * t:P * t + P])
                        return lambda k, t: h_tile(2 * u + k, t)

                    wide_unit(32, 22, m_tile(0), True, False)
                    pe.wait_ge(gate_sum, 6)
                    m_transposes(4)
                    wide_unit(33, 22, m_tile(1), False, False)
                    pe.wait_ge(xT_lo, 8)
                    wide_unit(34, 22, m_tile(2), False, False)
                    wide_unit(35, 22, m_tile(3), False, True)

                    keep_warm(20, 7)
                    pe.wait_ge(xn_dve, 2)
                    pe.wait_ge(xn_act, 2)
                    x_transposes(8)
                    pe.wait_ge(wr_lo_out, 1)
                    for c in range(C):
                        if c % 2 == 0:
                            pe.wait_ge(xT_lo, 8 + c // 2 + 1)
                        ins = three(ps[0:NG + NE, 0, 0:T], (wr_hi[:, c, :], wr_lo[:, c, :]), h_tile(c),
                                    c == 0, c == C - 1)
                    ins.then_inc(route_mm, 1)
                    pe.wait_ge(logitT_out, 1)
                    for t in range(TT):
                        ins = nc.tensor.transpose(ps[:, 1, 36 * t:36 * t + 36], logitT[:, P * t:P * t + P],
                                                  ident[0:NG + NE, 0:NG + NE])
                    ins.then_inc(logit_T, 1)
                    keep_warm(13, 7)
                    pe.wait_ge(member_ok, 1)
                    m0, m1 = member[:, 0:1, :], member[:, 1:2, :]
                    mm(ps[:, 2, 0:64], incl_T[:], member[:], start=True, stop=False, skip_group_check=True)
                    mm(ps[:, 2, 32:96], ones[:], m0.broadcast_to([P, 2, NE]), start=False, stop=False,
                       skip_group_check=True)
                    mm(ps[:, 2, 64:96], ones[:], m1, start=False, stop=True, skip_group_check=True)\
                        .then_inc(rank_mm, 1)
                    keep_warm(5, 7)
                    pe.wait_ge(passes_ok, 1)
                    pe.wait_ge(xs_lo, TT)
                    keep_warm(4, 7)
                    pe.sem_inc(gath_mm, 1)
                    pe.sem_inc(scat_T, 1)

                    passes = pe.alloc_register("pe_passes")
                    pe.reg_mov(passes, 0)

                    def scatter(n, k):
                        t, hf = k // 2, k % 2
                        if k == 0:
                            pe.wait_ge(y_act, 4 * n + 1)
                            pe.wait_ge(y_dve, 4 * n + 1)
                        if k >= 2:
                            pe.wait_ge(x_add, 4 * n + k - 1)
                        mm(ps[:, (7, 1)[hf], :], scatT[:, t, :], y_slots[:, 512 * hf:512 * hf + 512],
                           start=True, stop=True).then_inc(scat_mm, 1)

                    def expert_pass(main, g):
                        n = pe.snap(passes)
                        pe.wait_ge(pick_ok, n + 2)
                        for b in range(2):
                            for c in range(4):
                                cc = 4 * b + c
                                for t in range(TT):
                                    for part in (xn_hi, xn_lo):
                                        ins = mm(ps[:, b, P * c:P * c + P], part[:, t, P * cc:P * cc + P],
                                                 pick[:, t, :], start=(t == 0 and part is xn_hi),
                                                 stop=(t == 1 and part is xn_lo), skip_group_check=True)
                            ins.then_inc(gath_mm, 1)
                        pe.wait_ge(wpick_ok, n + 1)
                        pe.wait_ge(gath_out, 2 * n + 1)
                        for t in range(TT):
                            ins = nc.tensor.transpose(ps[:, 0, P * t:P * t + P], wpick[:, t, :], ident[:])
                        ins.then_inc(scat_T, 1)

                        def gate_up(i):
                            if i == 0:
                                pe.wait_ge(gath_out, 2 * n + 2)
                            for part in range(2):
                                arrived(3 * i + part)
                            w = ring[:, 3 * i * UNIT:(3 * i + 2) * UNIT]\
                                .rearrange("p (s c f) -> p s c f", s=2, c=C)
                            for c in range(C):
                                for j in range(4):
                                    ins = mm(ps[32 * j:32 * j + 32, 2 + i % 2, 0:P],
                                             hG[:, c, SLOTS * i:SLOTS * i + SLOTS], w[:, :, c, 64 * j:64 * j + 64],
                                             start=(c == 0), stop=(c == C - 1))
                            ins.then_inc(gu_mm, 1)

                        def arrived(s):
                            k = (LOADS_LOW * l + NU // MRING) if s < MRING else LOADS_HIGH * l
                            pe.wait_ge(ring_loaded[s], 16 * (k + g + 1))

                        def hidden(i):
                            pe.wait_ge(hid_out, 4 * n + i + 1)
                            for k in range(2):
                                ins = mm(ps[:, 4, SLOTS * k:SLOTS * k + SLOTS], hid[:, i % 2, k::2],
                                         ident[0:SLOTS, 0:SLOTS], start=True, stop=True)
                            ins.then_inc(hid_T, 1)

                        def down(i):
                            arrived(3 * i + 2)
                            pe.wait_ge(hidT_out, 4 * n + i + 1)
                            if i >= 2:
                                pe.wait_ge(y_act, 4 * n + i)
                                pe.wait_ge(y_dve, 4 * n + i)
                            w = slot(3 * i + 2).rearrange("p (k d) -> p k d", k=2)
                            for k in range(2):
                                for q in range(4):
                                    ins = mm(ps[32 * q:32 * q + 32, 5 + i % 2, 0:256], hidT[:, i % 2, k, :],
                                             w[:, k, 256 * q:256 * q + 256], start=(k == 0), stop=(k == 1))
                            ins.then_inc(down_mm, 1)

                        gate_up(0)
                        scatter(n, 0)
                        scatter(n, 1)
                        gate_up(1)
                        scatter(n, 2)
                        scatter(n, 3)
                        for i in range(GE):
                            hidden(i)
                            down(i)
                            if i + 2 < GE:
                                gate_up(i + 2)
                        pe.reg_add(passes, passes, 1)

                    with pe.Fori(0, GROUPS) as g:
                        p_ = pe.value_load(npass[0:1, bass.ds(g, 1)], min_val=1, max_val=MAXPASS)
                        with pe.If(p_ > 1):
                            with pe.Fori(1, p_):
                                expert_pass(False, g)
                        expert_pass(True, g)
                    done = pe.snap(passes)
                    for k in range(4):
                        scatter(done, k)
                    keep_warm(10, 3)

                @layer.scalar
                def _(act):
                    A = nc.scalar.activation

                    def hi(u):
                        s = u % MRING
                        act.wait_ge(ring_loaded[s], 16 * (LOADS_LOW * l + u // MRING + 1))
                        for v in (2 * u, 2 * u + 1):
                            if v >= SPLITS:
                                act.wait_ge(half_used, v - SPLITS + 1)
                            A(half_view(split_hi[:, v % SPLITS, :], v), raw_half(v), ACT.Copy).then_inc(hi_done, 1)

                    def block_evac(k, dst, b0, func=ACT.Copy, n=512):
                        act.wait_ge(half_used, 2 * LAST_UNIT[k] + 2)
                        A(dst, ps[:, b0:b0 + 2, 0:n], func).then_inc(block_out, 1)

                    def hi_half(v):
                        s = v // 2
                        act.wait_ge(ring_loaded[s], 16 * (LOADS_LOW * l + 1))
                        A(half_view(split_hi[:, v, :], v), raw_half(v), ACT.Copy).then_inc(hi_done, 1)

                    def normalise():
                        A(xnp[1], xp[1], ACT.Copy, scale=ir[:, 1:2]).then_inc(xn_act, 1)

                    def xT_hi_parts(k, g0, banks=range(4)):
                        act.wait_ge(small_ready, 1)
                        for b in banks:
                            act.wait_ge(xT_mm, k + b + 1)
                            for j in range(2):
                                c = 2 * b + j
                                ins = A(hT_hi[:, c, :], ps[:, 4 + b, T * j:T * j + T], ACT.Copy,
                                        scale=small[:, g0 + c:g0 + c + 1])
                            ins.then_inc(xT_hi, 1)

                    def yT_high(k, at, b0):
                        act.wait_ge(yT_mm, k)
                        A(yT_hi[:, at, :, :], ps[:, b0, :], ACT.Copy).then_inc(yT_hi_out, 1)

                    def p_evac(k, t, b0):
                        act.wait_ge(pT_mm, k)
                        A(pT[:, 0:t + 1, :, :], ps[:, b0:b0 + t + 1, :].rearrange("p b (h q) -> p b h q", h=NH),
                          ACT.Copy).then_inc(pT_out, 1)

                    def softplus(t):
                        w = P * (t + 1)
                        z, s_ = zc[:, :, 0:w], sc[:, :, 0:w]
                        act.wait_ge(zc_out, t + 1)
                        A(s_, z, ACT.Abs).then_inc(zabs, 1)
                        act.wait_ge(zabs, 2 * t + 1)
                        A(s_, s_, ACT.Exp, scale=-1.0).then_inc(zabs, 1)
                        act.wait_ge(zabs, 2 * t + 2)
                        A(s_, s_, ACT.Ln, bias=1.0).then_inc(zln, 1)

                    def stick_exp(t):
                        w = P * (t + 1)
                        act.wait_ge(zarg, t + 1)
                        A(zc[:, :, 0:w], zc[:, :, 0:w], ACT.Exp).then_inc(zexp, 1)

                    def softmax_exp(t, buf):
                        w = P * (t + 1)
                        act.wait_ge(la_max, t + 1)
                        for s_ in range(NH):
                            ins = A(buf[:, s_, 0:w], buf[:, s_, 0:w], ACT.Exp, bias=lneg[:, s_:s_ + 1],
                                    scale=ATT_SCALE, accum_out=lsum[:, s_:s_ + 1])
                        ins.then_inc(la_exp, 1)

                    normalise()
                    hi_half(0)
                    xT_hi_parts(0, PG1, (0, 1))
                    hi_half(1)
                    xT_hi_parts(0, PG1, (2, 3))
                    hi(1)
                    hi(2)
                    block_evac(0, vi[:, :, :], 0, n=420)
                    hi(3)
                    hi(4)
                    block_evac(1, uv[:, :, :], 2)
                    hi(5)
                    act.wait_ge(idx_T, 1)
                    act.wait_ge(first, 1)
                    for h in range(IH):
                        A(iqT[ID * h:ID * h + ID, h, :], ps[ID * h:ID * h + ID, 5, 0:T], ACT.Copy)
                    A(ikT, ps[:, 5, T:2 * T], ACT.Copy).then_inc(idx_out, 1)
                    hi(6)
                    block_evac(2, qkT_c.rearrange("p m t -> p (m t)").rearrange("p (a n) -> p a n", a=2), 0)
                    act.wait_ge(rel_mm, 1)
                    A(zc[:, 0:2, :], ps[:, 4, :], ACT.Relu).then_inc(rel_out, 1)
                    act.wait_ge(rel_mm, 2)
                    A(sc[:, :, :], ps[:, 6:8, :], ACT.Relu).then_inc(rel_out, 1)
                    hi(7)
                    act.wait_ge(qk_T, 1)
                    A(qkT_a, ps[:, 4:6, :], ACT.Copy).then_inc(qk_out, 1)
                    hi(8)
                    act.wait_ge(half_used, 2 * LAST_UNIT[3] + 2)
                    A(vc[:, :, :], ps[:, 2, :], ACT.Copy)
                    A(bdT, ps[:, 3, :], ACT.Copy).then_inc(block_out, 1)
                    hi(9)
                    softplus(0)
                    hi(10)
                    block_evac(4, cxT.rearrange("p m t -> p (m t)").rearrange("p (a n) -> p a n", a=2), 0)
                    hi(11)
                    act.wait_ge(conv_y, 1)
                    A(yT_hi[:, 0, :, :], cxT[:, 2:4, :], ACT.Copy).then_inc(yT_hi_out, 1)
                    hi(12)
                    block_evac(5, uv[:, :, :], 2, ACT.Gelu_apprx_tanh)
                    hi(13)
                    stick_exp(0)
                    block_evac(6, br[:, 0, :, :], 0)
                    block_evac(7, br[:, 1, :, :], 2)
                    act.wait_ge(ln_var, 1)
                    A(lsd, lvar, ACT.Sqrt).then_inc(ln_root, 1)
                    hi(14)
                    p_evac(1, 0, 6)
                    softplus(1)
                    hi(15)
                    stick_exp(1)
                    block_evac(8, sig[:, :, :], 0, ACT.Sigmoid)
                    hi(16)
                    p_evac(2, 1, 4)
                    yT_high(1, 1, 6)
                    hi(17)
                    act.wait_ge(gate_prod, 1)
                    block_evac(9, sig[:, :, :], 2, ACT.Sigmoid)
                    hi(18)
                    act.wait_ge(gate_prod, 2)
                    block_evac(10, br[:, 0, :, :], 0)
                    yT_high(2, 0, 5)
                    block_evac(11, br[:, 1, :, :], 2)
                    hi(19)
                    hi(20)
                    softmax_exp(0, sc)
                    block_evac(12, sig[:, :, :], 0, ACT.Sigmoid)
                    hi(21)
                    softmax_exp(1, zc)
                    hi(22)
                    p_evac(3, 0, 6)
                    act.wait_ge(gate_sum, 1)
                    block_evac(13, sig[:, :, :], 2, ACT.Sigmoid)
                    hi(23)
                    act.wait_ge(pv_mm, 3)
                    p_evac(4, 1, 4)
                    act.wait_ge(gate_prod, 4)
                    block_evac(14, br[:, 0, :, :], 0)
                    block_evac(15, br[:, 1, :, :], 2)
                    hi(24)
                    hi(25)
                    act.wait_ge(gate_sum, 2)
                    block_evac(16, sig[:, :, :], 0, ACT.Sigmoid)
                    hi(26)
                    yT_high(3, 1, 6)
                    hi(27)
                    act.wait_ge(gate_sum, 3)
                    block_evac(17, sig[:, :, :], 2, ACT.Sigmoid)
                    hi(28)
                    act.wait_ge(gate_prod, 6)
                    block_evac(18, br[:, 0, :, :], 0)
                    block_evac(19, br[:, 1, :, :], 2)
                    hi(29)
                    hi(30)
                    act.wait_ge(gate_sum, 4)
                    block_evac(20, sig[:, :, :], 0, ACT.Sigmoid)
                    hi(31)

                    def mT_high(k, dst, b0):
                        for b in range(2):
                            act.wait_ge(xT_mm, k + b + 1)
                            A(dst(b), ps[:, b0 + b, :], ACT.Copy).then_inc(xT_hi, 1)

                    mT_high(4, lambda b: yT_hi[:, b, :, :], 4)
                    hi(32)
                    act.wait_ge(gate_sum, 5)
                    block_evac(21, sig[:, :, :], 2, ACT.Sigmoid)
                    hi(33)
                    mT_high(6, lambda b: hT_hi[:, 4 + 2 * b:6 + 2 * b, :], 6)
                    hi(34)
                    hi(35)

                    act.wait_ge(half_used, 2 * NU - 1)
                    act.wait_ge(layer_loaded, 16 * 5 * (l + 1))
                    A(wr_hi, wr[:], ACT.Copy).then_inc(wr_hi_out, 1)
                    preload_sqrt()
                    for t in range(TT):
                        act.wait_ge(x_mid, t + 1)
                        square_of_x(t)
                    root_of_mean(act, 1)
                    act.wait_ge(inv_rms, 1)
                    normalise()
                    act.wait_ge(xn_act, 2)
                    A(xn_hi[:, 1, :], wide[:, 1, :], ACT.Copy).then_inc(xs_hi, 1)
                    xT_hi_parts(8, PG2)
                    act.wait_ge(route_mm, 1)
                    A(logitT, ps[0:NG + NE, 0, 0:T], ACT.Copy).then_inc(logitT_out, 1)
                    act.wait_ge(gmax, 1)
                    A(rt[:, 0:8], rt[:, 8:16], ACT.Exp).then_inc(gexp, 1)
                    act.wait_ge(emax, 1)
                    A(rt[:, 16:32], rt[:, 64:80], ACT.Exp).then_inc(eexp, 1)
                    act.wait_ge(passes_ok, 1)

                    passes = act.alloc_register("act_passes")
                    act.reg_mov(passes, 0)

                    def expert_pass(main):
                        n = act.snap(passes)
                        def silu_of(i):
                            act.wait_ge(gu_mm, 4 * n + i + 1)
                            if main:
                                act.sem_inc(unit_used, 2)
                            A(silu[:, i % 2, :], ps[:, 2 + i % 2, 0:64], ACT.Silu).then_inc(silu_out, 1)

                        silu_of(0)
                        act.wait_ge(scat_T, n + 2)
                        act.wait_ge(scat_mm, 4 * n + 4)
                        A(scatT, ps[:, 0, 0:2 * P], ACT.Copy)
                        silu_of(1)
                        for i in range(GE):
                            act.wait_ge(hid_T, 4 * n + i + 1)
                            A(hidT[:, i % 2, :, :], ps[:, 4, 0:2 * SLOTS], ACT.Copy).then_inc(hidT_out, 1)
                            act.wait_ge(down_mm, 4 * n + i + 1)
                            if main:
                                act.sem_inc(unit_used, 1)
                            for q in range(2):
                                ins = A(y_slots[SLOTS * i:SLOTS * i + SLOTS, 256 * q:256 * q + 256],
                                        ps[32 * q:32 * q + 32, 5 + i % 2, 0:256], ACT.Copy)
                            ins.then_inc(y_act, 1)
                            if i + 2 < GE:
                                silu_of(i + 2)
                        act.reg_add(passes, passes, 1)

                    with act.Fori(0, GROUPS) as g:
                        p_ = act.value_load(npass[0:1, bass.ds(g, 1)], min_val=1, max_val=MAXPASS)
                        with act.If(p_ > 1):
                            with act.Fori(1, p_):
                                expert_pass(False)
                        expert_pass(True)

                    preload_sqrt()
                    done = act.snap(passes)
                    for t in range(TT):
                        act.wait_ge(x_add, 4 * done + (2 * t + 2))
                        square_of_x(t)
                    root_of_mean(act, 2)

                @layer.vector
                def _(dve):
                    V = nc.vector
                    n = [0]

                    def link(ins):
                        n[0] += 1
                        ins.then_inc(dve_c, 1)
                        dve.wait_ge(dve_c, n[0])

                    def lo(u):
                        lo_half(2 * u)
                        lo_half(2 * u + 1)

                    def lo_half(v):
                        dve.wait_ge(hi_done, v + 1)
                        V.tensor_tensor(half_view(split_lo[:, v % SPLITS, :], v), raw_half(v),
                                        half_view(split_hi[:, v % SPLITS, :], v).bitcast(F32),
                                        ALU.subtract).then_inc(lo_done, 1)

                    def normalise():
                        V.tensor_scalar(xnp[0], xp[0], ir[:, 0:1], None, ALU.mult).then_inc(xn_dve, 1)

                    def xT_lo_parts(k, g0, banks=range(4)):
                        for b in banks:
                            dve.wait_ge(xT_hi, k + b + 1)
                            for j in range(2):
                                c = 2 * b + j
                                ins = V.scalar_tensor_tensor(hT_lo[:, c, :], ps[:, 4 + b, T * j:T * j + T],
                                                             small[:, g0 + c:g0 + c + 1],
                                                             hT_hi[:, c, :].bitcast(F32), ALU.mult, ALU.subtract)
                            ins.then_inc(xT_lo, 1)

                    def yT_low(k, at, b0):
                        dve.wait_ge(yT_hi_out, k)
                        V.tensor_tensor(yT_lo[:, at, :, :].rearrange("p k t -> p (k t)"), ps[:, b0, :],
                                        yT_hi[:, at, :, :].rearrange("p k t -> p (k t)").bitcast(F32),
                                        ALU.subtract).then_inc(yT_lo_out, 1)

                    def index_score(t):
                        w = P * (t + 1)
                        score = score_of[t]
                        dve.wait_ge(rel_out, t + 1)
                        for h in range(IH):
                            rel = zc[:, 0:2, :].rearrange("p a s -> p (a s)")[:, P * h:P * h + P] if t == 0 \
                                else sc[:, h, :]
                            prev = (mask_a[:, P:] if t == 0 else mask_a[:]) if h == 0 else score[:, 0:w]
                            link(V.scalar_tensor_tensor(score[:, 0:w], rel, vi[:, t, 416 + h:417 + h], prev,
                                                        ALU.mult, ALU.add))

                    def top_rounds(t, rounds):
                        w = P * (t + 1)
                        score = score_of[t]
                        for _ in range(rounds):
                            link(V.max(top8, score[:, 0:w]))
                            link(V.match_replace(score[:, 0:w], top8, score[:, 0:w], TAKEN))

                    def select_mask(t):
                        dst = score_of[t]
                        link(V.tensor_scalar(dst, dst, TAKEN / 1.5, MASKED, ALU.is_gt, ALU.mult))
                        link(V.tensor_tensor(dst, dst, mask_a[:, P:] if t == 0 else mask_a[:], ALU.add))

                    def stick_logits(t, b0):
                        w = P * (t + 1)
                        m = mask_c[:, P:] if t == 0 else mask_c[:]
                        dve.wait_ge(zc_mm, t + 1)
                        if t == 1:
                            dve.wait_ge(pT_mm, 1)
                        V.scalar_tensor_tensor(zc[:, :, 0:w],
                                               ps[:, b0:b0 + 2, :].rearrange("p b n -> p (b n)")
                                               .rearrange("p (h s) -> p h s", h=NH)[:, :, 0:w],
                                               ATT_SCALE, m.rearrange("p (o s) -> p o s", o=1)
                                               .broadcast_to([P, NH, w]), ALU.mult, ALU.add).then_inc(zc_out, 1)

                    def stick_weights(t):
                        w = P * (t + 1)
                        z, s_ = zc[:, :, 0:w], sc[:, :, 0:w]
                        dve.wait_ge(zln, t + 1)
                        link(V.scalar_tensor_tensor(s_, z, 0.0, s_, ALU.max, ALU.add))
                        for h in range(NH):
                            rev = sc[:, h, 0:w][:, ::-1]
                            ones_w = ones[:, 0:1].broadcast_to([P, w])
                            ins = V.tensor_tensor_scan(rev, ones_w, rev, 0.0, ALU.mult, ALU.add)
                        link(ins)
                        V.tensor_tensor(z, z, s_, ALU.subtract).then_inc(zarg, 1)

                    def conv():
                        dve.wait_ge(block_out, 5)
                        link(V.tensor_tensor(cxT[:, 0:2, :], cxT[:, 0:2, :], cxT[:, 2:4, :], ALU.mult))
                        for tap in (2, 1, 0):
                            d = 2 - tap
                            for k in range(2):
                                w_ = small[:, PCW + 3 * k + tap:PCW + 3 * k + tap + 1]
                                z, y = cxT[:, k, :], cxT[:, 2 + k, :]
                                if d == 0:
                                    ins = V.tensor_scalar(y, z, w_, None, ALU.mult)
                                else:
                                    ins = V.scalar_tensor_tensor(y[:, d:T], z[:, 0:T - d], w_, y[:, d:T],
                                                                 ALU.mult, ALU.add)
                            link(ins)
                        V.tensor_tensor(cxT[:, 2:4, :], cxT[:, 2:4, :], bdT, ALU.mult).then_inc(conv_y, 1)
                        dve.wait_ge(conv_y, 1)
                        dve.wait_ge(yT_hi_out, 1)
                        V.tensor_tensor(yT_lo[:, 0, :, :], cxT[:, 2:4, :], yT_hi[:, 0, :, :].bitcast(F32),
                                        ALU.subtract).then_inc(yT_lo_out, 1)

                    def ln_stats():
                        dve.wait_ge(block_out, 6)
                        for t in range(TT):
                            link(V.bn_stats(bn[:, t, :], uv[:, t, BW:]))
                            link(V.bn_aggr(lmv[:, t, :], bn[:, t, :]))
                        link(V.tensor_scalar(lvar, lmv[:, :, 1], EPS, None, ALU.add))
                        V.tensor_scalar(lrs, lvar, -0.5, None, ALU.mult).then_inc(ln_var, 1)

                    def ln_apply():
                        dve.wait_ge(ln_root, 1)
                        dve.wait_ge(ln_var, 1)
                        link(newton(link, lsd, lsd, lrs))
                        for t in range(TT):
                            ins = V.tensor_scalar(vn[:, t, :], uv[:, t, BW:], lmv[:, t, 0:1], lsd[:, t:t + 1],
                                                  ALU.subtract, ALU.mult)
                        ins.then_inc(vn_dve, 1)

                    def sgu_gate():
                        dve.wait_ge(sgu_mm, 1)
                        for g in range(NG):
                            cols = slice(HD * g, HD * g + HD)
                            ins = V.scalar_tensor_tensor(y_ab[:, :, cols],
                                                         ps[:, 6, P * g:P * g + P].rearrange("p (t f) -> p t f", t=TT),
                                                         small[:, PBS + g:PBS + g + 1], uv[:, :, cols],
                                                         ALU.add, ALU.mult)
                        ins.then_inc(yb_done, 1)

                    def y_evac_c(t):
                        dve.wait_ge(pv_mm, t + 1)
                        V.tensor_copy(y_c[:, t, :], ps[:, 7, 0:BW]).then_inc(y_out, 1)

                    def sparse_logits(t, b0, buf):
                        w = P * (t + 1)
                        m = mb[:, 0:P] if t == 0 else mb[:, P:]
                        dve.wait_ge(la_mm, t + 1)
                        link(V.tensor_tensor(buf[:, :, 0:w],
                                             ps[:, b0:b0 + 2, :].rearrange("p b n -> p (b n)")
                                             .rearrange("p (h s) -> p h s", h=NH)[:, :, 0:w],
                                             m.rearrange("p (o s) -> p o s", o=1).broadcast_to([P, NH, w]),
                                             ALU.add))
                        link(V.tensor_reduce(lmax, buf[:, :, 0:w], AX.X, ALU.max))
                        if t == 1:
                            dve.wait_ge(la_exp, 1)
                            link(V.reciprocal(scal[:, 52:56], lsum))
                        V.tensor_scalar(lneg, lmax, -ATT_SCALE, None, ALU.mult).then_inc(la_max, 1)

                    def y_evac_a(t):
                        dve.wait_ge(pv_mm, t + 3)
                        inv = scal[:, 52:56]
                        if t == 1:
                            dve.wait_ge(y_out, 3)
                            link(V.reciprocal(inv, lsum))
                        for r in range(2):
                            ins = V.tensor_tensor(
                                y_ab[:, t, :].rearrange("p (m r f) -> p r m f", m=2, r=2)[:, r],
                                ps[:, 7, 0:BW].rearrange("p (m r f) -> p r m f", m=2, r=2)[:, r],
                                inv[:, 2 * r:2 * r + 2].rearrange("p (m o) -> p m o", o=1)
                                .broadcast_to([P, 2, HD]), ALU.mult)
                        ins.then_inc(y_out, 1)

                    def gate(j, use):
                        hf = j % 2
                        dve.wait_ge(block_out, use + 1)
                        dst = merged[:, :, 512 * hf:512 * hf + 512] if j < 2 else sig[:]
                        V.tensor_tensor(dst, sig[:], br[:, hf, :, :], ALU.mult).then_inc(gate_prod, 1)

                    def mT_low(k, dst, hi_part, b0):
                        for b in range(2):
                            dve.wait_ge(xT_hi, k + b + 1)
                            V.tensor_tensor(dst(b), ps[:, b0 + b, :].rearrange("p (k t) -> p k t", k=2),
                                            hi_part(b).bitcast(F32), ALU.subtract).then_inc(xT_lo, 1)

                    dve.wait_ge(once_loaded, 16 * SMALL_LOADS)
                    V.tensor_copy(small[:], small_all[:, bass.ds(l, 1), :].rearrange("p o n -> p (o n)"))\
                        .then_inc(small_ready, 1)
                    normalise()
                    dve.wait_ge(small_ready, 1)
                    lo_half(0)
                    xT_lo_parts(0, PG1, (0, 1))
                    lo_half(1)
                    xT_lo_parts(0, PG1, (2, 3))
                    for u in range(1, 6):
                        lo(u)
                    dve.wait_ge(ws_T, 1)
                    V.tensor_tensor(wsT[:], bank(4).rearrange("p (g t) -> p g t", g=NG),
                                    incl_T[:].rearrange("p (o t) -> p o t", o=1).broadcast_to([P, NG, P]),
                                    ALU.mult).then_inc(ws_ready, 1)
                    lo(6)
                    index_score(0)
                    lo(7)
                    top_rounds(0, 4)
                    lo(8)
                    index_score(1)
                    top_rounds(0, 2)
                    lo(9)
                    stick_logits(0, 6)
                    top_rounds(0, TOPK // 8 - 6)
                    select_mask(0)
                    lo(10)
                    lo(11)
                    conv()
                    lo(12)
                    stick_weights(0)
                    lo(13)
                    ln_stats()
                    stick_logits(1, 4)
                    lo(14)
                    ln_apply()
                    stick_weights(1)
                    lo(15)
                    y_evac_c(0)
                    sgu_gate()
                    gate(0, 8)
                    lo(16)
                    yT_low(2, 1, 6)
                    top_rounds(1, 2)
                    lo(17)
                    y_evac_c(1)
                    gate(1, 9)
                    top_rounds(1, 1)
                    lo(18)
                    yT_low(3, 0, 5)
                    top_rounds(1, 2)
                    lo(19)
                    sparse_logits(0, 6, sc)
                    top_rounds(1, TOPK // 8 - 5)
                    select_mask(1)
                    lo(20)
                    sparse_logits(1, 4, zc)
                    gate(2, 12)
                    lo(21)
                    lo(22)
                    y_evac_a(0)
                    gate(3, 13)
                    lo(23)
                    lo(24)
                    lo(25)
                    y_evac_a(1)
                    gate(4, 16)
                    lo(26)
                    yT_low(4, 1, 6)
                    lo(27)
                    gate(5, 17)
                    lo(28)
                    lo(29)
                    lo(30)
                    gate(6, 20)
                    lo(31)
                    mT_low(4, lambda b: yT_lo[:, b, :, :], lambda b: yT_hi[:, b, :, :], 4)
                    lo(32)
                    gate(7, 21)
                    dve.wait_ge(gate_prod, 8)
                    m_ = merged[:, :, 512:1024]
                    V.tensor_tensor(m_, m_, sig[:], ALU.add).then_inc(gate_sum, 1)
                    lo(33)
                    mT_low(6, lambda b: hT_lo[:, 4 + 2 * b:6 + 2 * b, :], lambda b: hT_hi[:, 4 + 2 * b:6 + 2 * b, :], 6)
                    lo(34)
                    lo(35)
                    dve.wait_ge(wr_hi_out, 1)
                    V.tensor_tensor(wr_lo, wr[:], wr_hi.bitcast(F32), ALU.subtract).then_inc(wr_lo_out, 1)
                    for t in range(TT):
                        dve.wait_ge((mid_mm, half_used)[t], (1, 2 * NU)[t])
                        for hf in range(2):
                            xs = x[:, t, 512 * hf:512 * hf + 512]
                            ins = V.tensor_tensor(xs, xs, bank(2 * hf + t), ALU.add)
                        ins.then_inc(x_mid, 1)

                    inverse_rms(dve, link, 1)
                    dve.wait_ge(inv_rms, 1)
                    normalise()
                    dve.wait_ge(xn_dve, 2)
                    link(V.tensor_copy(xn_hi[:, 0, :], wide[:, 0, :]))
                    V.tensor_tensor(xn_lo[:, 0, :], wide[:, 0, :], xn_hi[:, 0, :].bitcast(F32), ALU.subtract)\
                        .then_inc(xs_lo, 1)
                    V.memset(rt[:, 96:112], -TAKEN)
                    xT_lo_parts(8, PG2)
                    dve.wait_ge(logit_T, 1)
                    bias = small[:, PBR:PBR + NG + NE].rearrange("p (o e) -> p o e", o=1)\
                        .broadcast_to([P, TT, NG + NE])
                    link(V.tensor_tensor(rl, ps[:, 1, 0:TT * 36].rearrange("p (t e) -> p t e", t=TT), bias, ALU.add))

                    def r2(k):
                        return rt[:, k:k + 2]

                    def r3(k, w):
                        return rt[:, k:k + 2 * w].rearrange("p (t e) -> p t e", t=TT)

                    def bc(ap, w):
                        return ap.rearrange("p (t o) -> p t o", o=1).broadcast_to([P, TT, w])

                    g_logit, top_g, place = rl[:, :, 0:NG], r2(160), r2(162)
                    link(V.tensor_reduce(top_g, g_logit, AX.X, ALU.max))
                    V.tensor_tensor(r3(8, NG), g_logit, bc(top_g, NG), ALU.subtract).then_inc(gmax, 1)
                    for t in range(TT):
                        ins = V.scalar_tensor_tensor(r3(32, NG)[:, t], rl[:, t, 0:NG], top_g[:, t:t + 1],
                                                     desc[:, EG - NG:], ALU.is_ge, ALU.mult)
                    link(ins)
                    link(V.tensor_reduce(place, r3(32, NG), AX.X, ALU.max))
                    link(V.tensor_tensor(r3(40, NG), r3(32, NG), bc(place, NG), ALU.is_equal))
                    sel = r3(40, NG).rearrange("p t (g o) -> p t g o", o=1).broadcast_to([P, TT, NG, EG])
                    link(V.tensor_tensor(prod32, rl[:, :, NG:].rearrange("p t (g e) -> p t g e", g=NG), sel,
                                         ALU.mult))
                    ing, ranked, two, rest, both = r3(48, EG), r3(80, EG), r3(96, EG), r3(112, EG), r3(128, EG)
                    link(V.tensor_reduce(ing, prod32.rearrange("p t g e -> p t e g"), AX.X, ALU.add))
                    for t in range(TT):
                        ins = V.max(ranked[:, t], ing[:, t])
                    link(ins)
                    V.tensor_tensor(r3(64, EG), ing, ranked[:, :, 0:1].broadcast_to([P, TT, EG]), ALU.subtract)\
                        .then_inc(emax, 1)
                    link(V.tensor_copy(two[:, :, 0:2], ranked[:, :, 0:2]))
                    for t in range(TT):
                        ins = V.match_replace(rest[:, t], two[:, t], ing[:, t], TAKEN)
                    link(ins)
                    link(V.tensor_tensor(both, ing, rest, ALU.is_gt))
                    m4 = member.rearrange("p t (g e) -> p t g e", g=NG)
                    both4 = both.rearrange("p t (o e) -> p t o e", o=1).broadcast_to([P, TT, NG, EG])
                    V.tensor_tensor(m4, sel, both4, ALU.mult).then_inc(member_ok, 1)
                    part, sum_g, sum_e = r3(144, EG), r2(164), r2(166)
                    dve.wait_ge(gexp, 1)
                    V.tensor_reduce(sum_g, r3(0, NG), AX.X, ALU.add)
                    dve.wait_ge(eexp, 1)
                    link(V.tensor_tensor(part, r3(16, EG), both, ALU.mult))
                    link(V.tensor_reduce(sum_e, part, AX.X, ALU.add))
                    link(V.tensor_tensor(sum_e, sum_e, sum_g, ALU.mult))
                    link(V.reciprocal(sum_e, sum_e))
                    link(V.tensor_tensor(part, part, bc(sum_e, EG), ALU.mult))
                    V.tensor_tensor(wt[:].rearrange("p t (g e) -> p t g e", g=NG), sel,
                                    part.rearrange("p t (o e) -> p t o e", o=1)
                                    .broadcast_to([P, TT, NG, EG]), ALU.mult)
                    dve.wait_ge(rank_mm, 1)
                    V.tensor_tensor(rankm[:], ps[:, 2, 0:64].rearrange("p (t e) -> p t e", t=TT), member,
                                    ALU.mult)
                    link(V.tensor_reduce(cnts, ps[:, 2, 64:96].rearrange("p (g e) -> p g e", e=GE), AX.X, ALU.max))
                    over = prod32.rearrange("p t g e -> p (t g e)").rearrange("p (g k) -> p g k", g=GROUPS)
                    link(V.tensor_tensor(over, cnts.rearrange("p (g o) -> p g o", o=1)
                                         .broadcast_to([P, GROUPS, MAXPASS]),
                                         limits[:].rearrange("p (o k) -> p o k", o=1)
                                         .broadcast_to([P, GROUPS, MAXPASS]), ALU.is_gt))
                    link(V.tensor_reduce(cnts, over, AX.X, ALU.add))
                    V.tensor_copy(npass[:], cnts[0:1, :]).then_inc(passes_ok, 1)

                    passes = dve.alloc_register("dve_passes")
                    dve.reg_mov(passes, 0)

                    def scatter_add(k_, k):
                        t, hf = k // 2, k % 2
                        dve.wait_ge(scat_mm, 4 * k_ + k + 1)
                        xs = x[:, t, 512 * hf:512 * hf + 512]
                        V.tensor_tensor(xs, xs, bank((7, 1)[hf]), ALU.add).then_inc(x_add, 1)

                    def expert_pass():
                        k_ = dve.snap(passes)
                        for b in range(2):
                            dve.wait_ge(gath_mm, 2 * k_ + b + 2)
                            V.tensor_tensor(hG[:, 4 * b:4 * b + 4, :],
                                            bank(b).rearrange("p (c s) -> p c s", c=4),
                                            small[:, PG2 + 4 * b:PG2 + 4 * b + 4].rearrange("p (c o) -> p c o", o=1)
                                            .broadcast_to([P, 4, P]), ALU.mult).then_inc(gath_out, 1)

                        def hidden(i):
                            dve.wait_ge(silu_out, 4 * k_ + i + 1)
                            for j in range(4):
                                ins = V.tensor_tensor(hid[:, i % 2, 64 * j:64 * j + 64],
                                                      silu[32 * j:32 * j + 32, i % 2, :],
                                                      ps[32 * j:32 * j + 32, 2 + i % 2, 64:128], ALU.mult)
                            ins.then_inc(hid_out, 1)

                        hidden(0)
                        scatter_add(k_, 0)
                        scatter_add(k_, 1)
                        hidden(1)
                        dve.wait_ge(diff_ok, k_ + 2)
                        V.tensor_scalar(pick, place_diff, 0.0, None, ALU.is_equal).then_inc(pick_ok, 1)
                        scatter_add(k_, 2)
                        scatter_add(k_, 3)
                        for i in range(GE):
                            dve.wait_ge(down_mm, 4 * k_ + i + 1)
                            for q in (2, 3):
                                ins = V.tensor_copy(y_slots[SLOTS * i:SLOTS * i + SLOTS, 256 * q:256 * q + 256],
                                                    ps[32 * q:32 * q + 32, 5 + i % 2, 0:256])
                            ins.then_inc(y_dve, 1)
                            if i + 2 < GE:
                                hidden(i + 2)
                        dve.reg_add(passes, passes, 1)

                    dve.wait_ge(diff_ok, 1)
                    V.tensor_scalar(pick, place_diff, 0.0, None, ALU.is_equal).then_inc(pick_ok, 1)
                    with dve.Fori(0, GROUPS) as g:
                        p_ = dve.value_load(npass[0:1, bass.ds(g, 1)], min_val=1, max_val=MAXPASS)
                        with dve.If(p_ > 1):
                            with dve.Fori(1, p_):
                                expert_pass()
                        expert_pass()
                    done = dve.snap(passes)
                    for k in range(4):
                        scatter_add(done, k)

                    inverse_rms(dve, link, 2)

            nc.gpsimd.sem_clear(range(first.num, last.num + 1))
            nc.all_engine_barrier()

        gain = br[:, 0, :, :].rearrange("p a n -> p (a n)")
        with nc.Block() as final:

            @final.sync
            def _(sp):
                sp.dma_start(gain, norm_f_g.rearrange("(o n) -> o n", o=1).broadcast_to([P, D]))\
                    .then_inc(once_loaded, 16)
                out_v = out[0].rearrange("(t p) d -> t p d", p=P)
                for t in range(TT):
                    sp.wait_ge(x_mid, t + 1)
                    sp.dma_start(out_v[t], wide[:, t, :]).then_inc(out_stored, 16)
                sp.wait_ge(out_stored, 16 * TT)

            @final.vector
            def _(dve):
                V = nc.vector
                dve.wait_ge(once_loaded, 16 * (SMALL_LOADS + 1))
                for t in range(TT):
                    V.scalar_tensor_tensor(wide[:, t, :], x[:, t, :], ir[:, t:t + 1], gain, ALU.mult, ALU.mult)\
                        .then_inc(x_mid, 1)


_INS = ["x", "positions", "norm1_g", "w_in", "sgu_ln_g", "sgu_ln_b", "w_spatial", "b_spatial", "conv_w",
        "w_branch", "w_out", "norm2_g", "w_router_group", "b_router_group", "w_router_expert",
        "b_router_expert", "w_exp_gate", "w_exp_up", "w_exp_down", "norm_f_g"]


def kernel(**inputs):
    import numpy as _np
    import concourse.bacc as _bacc
    from concourse import mybir as _mybir
    from concourse.bass_utils import run_bass_kernel_spmd as _run

    nc = _bacc.Bacc("TRN2", target_bir_lowering=False, num_devices=1)
    arrays, args = {}, []
    for name in _INS:
        a = _np.ascontiguousarray(inputs[name])
        arrays[f"in_{name}"] = a
        args.append(nc.dram_tensor(f"in_{name}", a.shape, _mybir.dt.from_np(a.dtype), kind="ExternalInput").ap())
    args.append(nc.dram_tensor("out_0", (1, T, D), F32, kind="ExternalOutput").ap())
    build(nc, *args)
    r = _run(nc, [arrays], core_ids=[0])
    return r.results[0]["out_0"]
```
